# Optimizing a Trainium2 kernel written in Bass

```python
import math
import jax
import jax.numpy as jnp
from jax import lax
import numpy as np

D_MODEL = 1024
BATCH = 1
SEQ = 2048
DEPTH = 1

CHUNK = 64
N_META = 16
D_MIX = 2 * D_MODEL
SB_WIDTH = D_MIX // 2
SB_HEAD_DIM = 64
SB_HEADS = SB_WIDTH // SB_HEAD_DIM
SB_QBLOCK = 128
SSD_WIDTH = D_MIX - SB_WIDTH
SSD_HEAD_DIM = 64
SSD_HEADS = SSD_WIDTH // SSD_HEAD_DIM
SSD_GROUPS = 2
SSD_HEADS_PER_GROUP = SSD_HEADS // SSD_GROUPS
SSD_STATE = 128
SSD_CONV = 4
SSD_XBC = SSD_WIDTH + 2 * SSD_GROUPS * SSD_STATE
IN_WIDTHS = (SB_WIDTH, SB_WIDTH, SB_WIDTH, SB_WIDTH, SSD_WIDTH, SSD_XBC, SSD_HEADS)
D_IN = sum(IN_WIDTHS)
EPS = 1e-5
DT_MIN = 1e-3
DT_MAX = 1e-1

kernel_name = "hybrid_stickbreak_ssd_block"

def rms_norm(x, w):
    xf = x.astype(jnp.float32)
    y = xf * lax.rsqrt(jnp.mean(xf * xf, axis=-1, keepdims=True) + EPS)
    return (y * w.astype(jnp.float32)).astype(x.dtype)

def split_cols(proj):
    outs = []
    start = 0
    for width in IN_WIDTHS:
        outs.append(proj[..., start:start + width])
        start += width
    return outs

def causal_depthwise_conv(x, w, b):
    c = x.shape[-1]
    y = lax.conv_general_dilated(
        x, w[:, None, :].astype(x.dtype), window_strides=(1,),
        padding=[(SSD_CONV - 1, 0)], dimension_numbers=("NWC", "WIO", "NWC"),
        feature_group_count=c)
    return y + b.astype(x.dtype)

def stick_breaking_attention(q, k, v):
    seqlen = q.shape[1]
    scale = 1.0 / math.sqrt(q.shape[-1])
    outs = []
    for q0 in range(0, seqlen, SB_QBLOCK):
        q1 = min(q0 + SB_QBLOCK, seqlen)
        qb = q[:, q0:q1]
        kb = k[:, :q1]
        vb = v[:, :q1]
        z = jnp.einsum("bqhd,bkhd->bhqk", qb, kb).astype(jnp.float32) * scale
        t_pos = jnp.arange(q0, q1)[:, None]
        s_pos = jnp.arange(q1)[None, :]
        strict = s_pos < t_pos
        log_keep = jnp.where(strict, jax.nn.log_sigmoid(-z), 0.0)
        after = lax.cumsum(log_keep, axis=3, reverse=True) - log_keep
        weights = jnp.where(strict, jnp.exp(jax.nn.log_sigmoid(z) + after), 0.0)
        outs.append(jnp.einsum("bhqk,bkhd->bqhd", weights.astype(v.dtype), vb))
    return jnp.concatenate(outs, axis=1)

def ssd_chunked(xs, dt, a, bmat, cmat, d_skip):
    f32 = jnp.float32
    bsz, seqlen, _ = xs.shape
    pad = (-seqlen) % CHUNK
    G, R, P, N = SSD_GROUPS, SSD_HEADS_PER_GROUP, SSD_HEAD_DIM, SSD_STATE
    x = xs.astype(f32).reshape(bsz, seqlen, SSD_HEADS, P)
    bm = bmat.astype(f32).reshape(bsz, seqlen, G, N)
    cm = cmat.astype(f32).reshape(bsz, seqlen, G, N)

    def front(t):
        return jnp.pad(t, ((0, 0), (pad, 0)) + ((0, 0),) * (t.ndim - 2))

    x, dt, bm, cm = front(x), front(dt), front(bm), front(cm)
    lp = seqlen + pad
    nc = lp // CHUNK
    x = x.reshape(bsz, nc, CHUNK, G, R, P)
    dt = dt.reshape(bsz, nc, CHUNK, G, R)
    bm = bm.reshape(bsz, nc, CHUNK, G, N)
    cm = cm.reshape(bsz, nc, CHUNK, G, N)

    xdt = x * dt[..., None]
    a_cum = jnp.cumsum(dt * a.reshape(G, R), axis=2)
    seg = a_cum[:, :, :, None] - a_cum[:, :, None]
    causal = jnp.tril(jnp.ones((CHUNK, CHUNK), bool))[:, :, None, None]
    decay_ls = jnp.exp(jnp.where(causal, seg, -jnp.inf))
    cb = jnp.einsum("bclgn,bcsgn->bclsg", cm, bm)
    y_diag = jnp.einsum("bclsg,bclsgr,bcsgrp->bclgrp", cb, decay_ls, xdt)
    decay_to_end = jnp.exp(a_cum[:, :, -1:] - a_cum)
    states = jnp.einsum("bclgn,bclgr,bclgrp->bcgrpn", bm, decay_to_end, xdt)
    chunk_decay = jnp.exp(a_cum[:, :, -1])

    def step(h, inp):
        st, dec = inp
        return h * dec[..., None, None] + st, h

    h0 = jnp.zeros((bsz, G, R, P, N), f32)
    _, h_start = lax.scan(step, h0, (jnp.moveaxis(states, 1, 0), jnp.moveaxis(chunk_decay, 1, 0)))
    h_start = jnp.moveaxis(h_start, 0, 1)
    y_off = jnp.einsum("bclgn,bcgrpn,bclgr->bclgrp", cm, h_start, jnp.exp(a_cum))
    y = y_diag + y_off + x * d_skip.astype(f32).reshape(G, R)[:, :, None]
    y = y.reshape(bsz, lp, SSD_WIDTH)[:, pad:]
    return y.astype(xs.dtype)

def hybrid_layer(h, norm_w, w_in, conv_w, conv_b, dt_bias, a_log, d_skip, sb_norm_w, ssd_norm_w, w_out):
    bsz, seqlen, _ = h.shape
    u = rms_norm(h, norm_w)
    proj = jnp.einsum("bld,de->ble", u, w_in)
    q, k, v, sb_gate, ssd_z, xbc, dt_raw = split_cols(proj)
    hs = (bsz, seqlen, SB_HEADS, SB_HEAD_DIM)
    o_sb = stick_breaking_attention(q.reshape(hs), k.reshape(hs), v.reshape(hs))
    o_sb = o_sb.reshape(bsz, seqlen, SB_WIDTH)
    y_sb = rms_norm(o_sb * jax.nn.silu(sb_gate), sb_norm_w)
    xbc = jax.nn.silu(causal_depthwise_conv(xbc, conv_w, conv_b))
    xs = xbc[..., :SSD_WIDTH]
    bmat = xbc[..., SSD_WIDTH:SSD_WIDTH + SSD_GROUPS * SSD_STATE]
    cmat = xbc[..., SSD_WIDTH + SSD_GROUPS * SSD_STATE:]
    dt = jax.nn.softplus(dt_raw.astype(jnp.float32) + dt_bias.astype(jnp.float32))
    a = -jnp.exp(a_log.astype(jnp.float32))
    o_ssd = ssd_chunked(xs, dt, a, bmat, cmat, d_skip)
    y_ssd = rms_norm(o_ssd * jax.nn.silu(ssd_z), ssd_norm_w)
    y = jnp.concatenate([y_sb, y_ssd], axis=-1)
    return h + jnp.einsum("ble,ed->bld", y, w_out)

def setup_inputs(seed: int = 0) -> dict:
    key = jax.random.key(seed)
    ks = jax.random.split(key, 13)
    nrm = jax.random.normal
    x = nrm(ks[0], (BATCH, SEQ, D_MODEL), jnp.float32)
    meta_tokens = nrm(ks[1], (N_META, D_MODEL), jnp.float32)
    norm_w = 1.0 + 0.02 * nrm(ks[2], (DEPTH, D_MODEL), jnp.float32)
    w_in = nrm(ks[3], (DEPTH, D_MODEL, D_IN), jnp.float32) * D_MODEL ** -0.5
    conv_w = nrm(ks[4], (DEPTH, SSD_CONV, SSD_XBC), jnp.float32) * SSD_CONV ** -0.5
    conv_b = 0.02 * nrm(ks[5], (DEPTH, SSD_XBC), jnp.float32)
    dt0 = jnp.exp(jax.random.uniform(ks[6], (DEPTH, SSD_HEADS), jnp.float32,
                                     minval=math.log(DT_MIN), maxval=math.log(DT_MAX)))
    dt_bias = dt0 + jnp.log(-jnp.expm1(-dt0))
    a_log = jnp.log(jax.random.uniform(ks[7], (DEPTH, SSD_HEADS), jnp.float32, minval=1.0, maxval=16.0))
    d_skip = 1.0 + 0.1 * nrm(ks[8], (DEPTH, SSD_HEADS), jnp.float32)
    sb_norm_w = 1.0 + 0.02 * nrm(ks[9], (DEPTH, SB_WIDTH), jnp.float32)
    ssd_norm_w = 1.0 + 0.02 * nrm(ks[10], (DEPTH, SSD_WIDTH), jnp.float32)
    w_out = nrm(ks[11], (DEPTH, D_MIX, D_MODEL), jnp.float32) * D_MIX ** -0.5
    final_norm_w = 1.0 + 0.02 * nrm(ks[12], (D_MODEL,), jnp.float32)
    return {"x": x, "meta_tokens": meta_tokens, "norm_w": norm_w, "w_in": w_in,
            "conv_w": conv_w, "conv_b": conv_b, "dt_bias": dt_bias, "a_log": a_log,
            "d_skip": d_skip, "sb_norm_w": sb_norm_w, "ssd_norm_w": ssd_norm_w,
            "w_out": w_out, "final_norm_w": final_norm_w}

def reference(x, meta_tokens, norm_w, w_in, conv_w, conv_b, dt_bias, a_log, d_skip,
              sb_norm_w, ssd_norm_w, w_out, final_norm_w):
    bsz = x.shape[0]
    meta = jnp.broadcast_to(meta_tokens.astype(x.dtype)[None], (bsz, N_META, D_MODEL))
    h = jnp.concatenate([meta, x], axis=1)
    for layer in range(DEPTH):
        h = hybrid_layer(h, norm_w[layer], w_in[layer], conv_w[layer], conv_b[layer],
                         dt_bias[layer], a_log[layer], d_skip[layer], sb_norm_w[layer],
                         ssd_norm_w[layer], w_out[layer])
    h = rms_norm(h, final_norm_w)
    return h[:, N_META:]


_drawn_inputs = setup_inputs


def setup_inputs(seed=0):
    import zlib

    import numpy as np

    out = dict(_drawn_inputs(seed))
    spreads = {}
    factors = {'meta_tokens': 2.964,
     'conv_b': 3.799,
     'sb_norm_w': 5.717,
     'ssd_norm_w': 5.745,
     'final_norm_w': 2.892}
    for name, (base, spread) in spreads.items():
        noise = np.random.default_rng([zlib.crc32(name.encode()), seed]).standard_normal(out[name].shape)
        drawn = base * np.exp(spread * noise) if base else spread * noise
        out[name] = jnp.asarray(drawn.astype(out[name].dtype))
    for name, factor in factors.items():
        out[name] = (out[name] * factor).astype(out[name].dtype)
    return out
```

```python
from contextlib import ExitStack

import concourse.bass as bass
from concourse import mybir

ALU = mybir.AluOpType
ACT = mybir.ActivationFunctionType
F32 = mybir.dt.float32
F32R = mybir.dt.float32r
BF16 = mybir.dt.bfloat16

P = 128
D = 1024
KB = D // P
SEQ = 2048
META = 16
T = META + SEQ
NT = SEQ // P
W = 512
NW = SEQ // W
HEAD = 64
HEADS = 16
PAIRS = HEADS // 2
STATE = 128
GROUPS = 2
HPG = HEADS // GROUPS
CONV = 4
XBC = D + 2 * GROUPS * STATE
XB = XBC // P
EPS = 1e-5
START = 4
K_BLOCK, X_BLOCK = 0, PAIRS
Q_BLOCK = X_BLOCK + XB
G_BLOCK = Q_BLOCK + PAIRS
V_BLOCK = G_BLOCK + 2 * KB
MB = 2 * KB
CHUNKS = [(0, META)] + [(META + W * c, W) for c in range(NW)]
EXP_AND_LN = "natural_log_exp_and_others"
Q_SCALE = HEAD ** -0.5
NEVER = -(2.0 ** 100)
LN_TOP = float(2 ** 60)


class Memory:

    def __init__(self, nc, ctx):
        self.nc, self.ctx, self.semaphores = nc, ctx, []
        ctx.callback(self.clear)

    def start(self):
        nc = self.nc
        engines = (nc.sync, nc.gpsimd, nc.scalar, nc.vector, nc.tensor)
        for n, sem in enumerate(self.semaphores):
            engines[n % len(engines)].sem_inc(sem, START)
        nc.all_engine_barrier()

    def clear(self):
        self.nc.clear_and_free_semaphores(self.semaphores)
        self.nc.all_engine_barrier()

    def sbuf(self, name, shape, dt=F32):
        return self.ctx.enter_context(self.nc.sbuf_tensor(name, shape, dt))

    def psum(self, name, shape, dt=F32):
        return self.ctx.enter_context(self.nc.psum_tensor(name, shape, dt))

    def sem(self, name):
        self.semaphores.append(self.nc.alloc_semaphore(name))
        return self.semaphores[-1]

    def sems(self, name, n):
        return [self.sem(f"{name}_{i}") for i in range(n)]


def spread(column_block, n):
    return column_block.unsqueeze(2).to_broadcast([column_block.shape[0], column_block.shape[1], n])


def norm_stage(nc, x, meta, norm_w, ut_hi, ut_lo):
    with ExitStack() as ctx:
        m = Memory(nc, ctx)
        ident = m.sbuf("n_ident", [P, P])
        nw = m.sbuf("n_nw", [P, KB])
        power = m.sbuf("n_power", [P, 1])
        xin = [m.sbuf(f"n_xin{s}", [P, D]) for s in range(2)]
        squares = [m.sbuf(f"n_squares{s}", [P, D]) for s in range(2)]
        xn = [m.sbuf(f"n_xn{s}", [P, D]) for s in range(2)]
        un = [m.sbuf(f"n_un{s}", [P, KB, P]) for s in range(2)]
        ssq = [m.sbuf(f"n_ssq{s}", [P, 1]) for s in range(2)]
        var = [m.sbuf(f"n_var{s}", [P, 1]) for s in range(2)]
        rstd = [m.sbuf(f"n_rstd{s}", [P, 1]) for s in range(2)]
        pt = [m.psum(f"n_pt{s}", [P, KB, P]) for s in range(2)]
        nw_loaded, ident_zero, ident_ready = m.sem("nw_loaded"), m.sem("ident_zero"), m.sem("ident_ready")
        x_loaded = m.sems("x_loaded", 2)
        ssq_ready = m.sems("ssq_ready", 2)
        var_ready = m.sems("var_ready", 2)
        rstd_ready = m.sems("rstd_ready", 2)
        xn_ready = m.sems("xn_ready", 2)
        turned = m.sems("turned", 2)
        un_ready = m.sems("un_ready", 2)
        hi_ready = m.sems("hi_ready", 2)
        lo_ready = m.sems("lo_ready", 2)
        m.start()
        block = ctx.enter_context(nc.Block())

        @block.sync
        def _(sp):
            sp.dma_start(nw[:, :], norm_w).then_inc(nw_loaded, 16)

            def load(s, k, src, rows):
                sp.wait_ge(xn_ready[s], k + START)
                sp.dma_start(xin[s][0:rows, :], src).then_inc(x_loaded[s], 16)

            with sp.Fori(0, NT // 2) as i:
                for s in range(2):
                    load(s, i, x[0, bass.ds((2 * i + s) * P, P), :], P)
            load(0, NT // 2, meta[:, :], META)

        @block.gpsimd
        def _(pool):
            nc.gpsimd.memset(ident[:, :], 0.0).then_inc(ident_zero, 1)
            nc.gpsimd.memset(power[:, :], -0.5).then_inc(ident_zero, 1)
            pool.wait_ge(ident_zero, START + 2)
            nc.gpsimd.affine_select(out=ident[:, :], in_=ident[:, :], compare_op=ALU.not_equal, fill=1.0,
                                    base=0, pattern=[[-1, P]], channel_multiplier=1).then_inc(ident_ready, 1)

            def root(s, k, rows):
                pool.wait_ge(var_ready[s], k + 1 + START)
                nc.gpsimd.tensor_tensor(rstd[s][0:rows, :], var[s][0:rows, :], power[0:rows, :],
                                        ALU.pow).then_inc(rstd_ready[s], 1)

            with pool.Fori(0, NT // 2) as i:
                for s in range(2):
                    root(s, i, P)
            root(0, NT // 2, META)

        @block.scalar
        def _(act):
            def square(s, k, rows):
                act.wait_ge(x_loaded[s], 16 * (k + 1) + START)
                nc.scalar.activation(squares[s][0:rows, :], xin[s][0:rows, :], ACT.Square,
                                     accum_out=ssq[s][0:rows, :]).then_inc(ssq_ready[s], 1)

            def high(s, k, col, n):
                act.wait_ge(un_ready[s], k + 1 + START)
                nc.scalar.copy(ut_hi[:, :, col:col + n] if isinstance(col, int) else ut_hi[:, :, bass.ds(col, n)],
                               un[s][:, :, 0:n]).then_inc(hi_ready[s], 1)

            with act.Fori(0, NT // 2) as i:
                for s in range(2):
                    square(s, i, P)
                for s in range(2):
                    high(s, i, META + (2 * i + s) * P, P)
            square(0, NT // 2, META)
            high(0, NT // 2, 0, META)

        @block.vector
        def _(dve):
            def variance(s, k, rows):
                dve.wait_ge(ssq_ready[s], k + 1 + START)
                nc.vector.tensor_scalar(var[s][0:rows, :], ssq[s][0:rows, :], 1.0 / D, EPS,
                                        ALU.mult, ALU.add).then_inc(var_ready[s], 1)

            def normalise(s, k, rows):
                dve.wait_ge(rstd_ready[s], k + 1 + START)
                dve.wait_ge(turned[s], k + START)
                nc.vector.tensor_scalar(xn[s][0:rows, :], xin[s][0:rows, :], rstd[s][0:rows, :], None,
                                        ALU.mult).then_inc(xn_ready[s], 1)

            def weigh(s, k, n):
                dve.wait_ge(turned[s], k + 1 + START)
                dve.wait_ge(lo_ready[s], k + START)
                nc.vector.tensor_tensor(un[s][:, :, 0:n], pt[s][:, :, 0:n], spread(nw[:, :], n),
                                        ALU.mult).then_inc(un_ready[s], 1)

            def low(s, k, col, n):
                hi = ut_hi[:, :, col:col + n] if isinstance(col, int) else ut_hi[:, :, bass.ds(col, n)]
                lo = ut_lo[:, :, col:col + n] if isinstance(col, int) else ut_lo[:, :, bass.ds(col, n)]
                dve.wait_ge(hi_ready[s], k + 1 + START)
                nc.vector.tensor_tensor(lo, un[s][:, :, 0:n], hi.bitcast(F32), ALU.subtract).then_inc(lo_ready[s], 1)

            dve.wait_ge(nw_loaded, START + 16)
            with dve.Fori(0, NT // 2) as i:
                for s in range(2):
                    variance(s, i, P)
                for s in range(2):
                    normalise(s, i, P)
                for s in range(2):
                    weigh(s, i, P)
                for s in range(2):
                    low(s, i, META + (2 * i + s) * P, P)
            variance(0, NT // 2, META)
            normalise(0, NT // 2, META)
            weigh(0, NT // 2, META)
            low(0, NT // 2, 0, META)

        @block.tensor
        def _(pe):
            pe.wait_ge(ident_ready, START + 1)

            def turn(s, k, rows):
                pe.wait_ge(xn_ready[s], k + 1 + START)
                pe.wait_ge(un_ready[s], k + START)
                for b in range(KB):
                    last = nc.tensor.transpose(pt[s][:, b, 0:rows], xn[s][0:rows, b * P:(b + 1) * P],
                                               ident[0:rows, 0:rows])
                last.then_inc(turned[s], 1)

            with pe.Fori(0, NT // 2) as i:
                for s in range(2):
                    turn(s, i, P)
            turn(0, NT // 2, META)


def feature_stage(nc, w_blocks, conv_wb, ut_hi, ut_lo, scratch):
    with ExitStack() as ctx:
        m = Memory(nc, ctx)
        LEAD = CONV
        NC = len(CHUNKS)
        LAST = NC - 1
        stage = [m.sbuf(f"f_stage{s}", [P, KB, P]) for s in range(2)]
        w_hi = [m.sbuf(f"f_w_hi{s}", [P, KB, P], F32R) for s in range(2)]
        w_lo = [m.sbuf(f"f_w_lo{s}", [P, KB, P], F32R) for s in range(2)]
        row_a = [m.sbuf(f"f_row_a{s}", [P, LEAD + T]) for s in range(2)]
        row_b = [m.sbuf(f"f_row_b{s}", [P, LEAD + T]) for s in range(2)]
        zero = m.sbuf("f_zero", [P, 1])
        taps = [m.sbuf(f"f_taps{s}", [P, CONV + 1]) for s in range(2)]
        acc = [m.psum(f"f_acc{c}", [P, W]) for c in range(NC)]
        w_loaded = m.sems("w_loaded", 2)
        w_split = m.sems("w_split", 2)
        acc_ready = [m.sems(f"acc_ready{s}", NC) for s in range(2)]
        acc_high = [m.sems(f"acc_high{s}", NC) for s in range(2)]
        acc_freed = [m.sems(f"acc_freed{s}", NC) for s in range(2)]
        taps_loaded = m.sems("taps_loaded", 2)
        lead_zero, zeroed = m.sem("lead_zero"), m.sem("zeroed")
        conv_step = m.sems("conv_step", 2)
        silu_done = m.sems("silu_done", 2)
        stored = m.sems("f_stored", 2)
        m.start()
        block = ctx.enter_context(nc.Block())

        KINDS = [("k", K_BLOCK, PAIRS, 0, ("k_hi", "k_lo")), ("conv", X_BLOCK, XB, 0, ("xbc",)),
                 ("q", Q_BLOCK, PAIRS, 1, ("q_hi", "q_lo")), ("gate", G_BLOCK, MB, 1, ("gate",))]
        TOTAL = V_BLOCK

        def stores_before(kind):
            done = 0
            for name, _, n, _, outs in KINDS:
                if name == kind:
                    return done
                done += n // 2 * len(outs)
            return done

        @block.sync
        def _(sp):
            def load(s, number):
                sp.dma_start(stage[s][:, :, :], w_blocks[bass.ds(number, 1), :, :, :]
                             .rearrange("b p k c -> (b p) k c")).then_inc(w_loaded[s], 16)

            load(0, 0)
            load(1, 1)
            for kind, b0, n, c0, outs in KINDS:
                first = CHUNKS[c0][0]

                def step(i, s, more):
                    j = i + b0 // 2
                    if kind == "conv":
                        sp.wait_ge(silu_done[s], i + 1 + START)
                    else:
                        sp.wait_ge(acc_freed[s][LAST], j + 1 + START)
                    for name, row in zip(outs, (row_a[s], row_b[s])):
                        sp.dma_start(scratch[name][bass.ds(i * 2 + s, 1), :, :].rearrange("b p t -> (b p) t"),
                                     row[:, LEAD + first:LEAD + T]).then_inc(stored[s], 16)
                    if more:
                        sp.wait_ge(w_split[s], (j + 1) * 2 + START)
                        load(s, i * 2 + (b0 + s + 2))

                peel = kind == KINDS[-1][0]
                with sp.Fori(0, n // 2 - peel) as i:
                    for s in range(2):
                        step(i, s, True)
                if peel:
                    for s in range(2):
                        step(n // 2 - 1, s, False)
            for s in range(2):
                sp.wait_ge(stored[s], 16 * (stores_before("gate") + MB // 2) + START)

        @block.gpsimd
        def _(pool):
            for s in range(2):
                nc.gpsimd.memset(row_a[s][:, 0:LEAD], 0.0).then_inc(lead_zero, 1)
            nc.gpsimd.memset(zero[:, :], 0.0).then_inc(zeroed, 1)
            pool.wait_ge(zeroed, START + 1)
            with pool.Fori(0, TOTAL // 2) as j:
                for s in range(2):
                    pool.wait_ge(w_loaded[s], j * 16 + 16 + START)
                    pool.wait_ge(acc_ready[s][LAST], j + START)
                    nc.gpsimd.tensor_tensor(w_hi[s][:, :, :], stage[s][:, :, :],
                                            spread(zero[:, :], P).to_broadcast([P, KB, P]), ALU.add).then_inc(w_split[s], 1)
                    pool.wait_ge(w_split[s], j * 2 + 1 + START)
                    nc.gpsimd.tensor_tensor(w_lo[s][:, :, :], stage[s][:, :, :], w_hi[s][:, :, :].bitcast(F32),
                                            ALU.subtract).then_inc(w_split[s], 1)

        @block.tensor
        def _(pe):
            for kind, b0, n, c0, _ in KINDS:
                with pe.Fori(0, n // 2) as i:
                    for s in range(2):
                        j = i + b0 // 2
                        pe.wait_ge(w_split[s], j * 2 + 2 + START)
                        for c in range(c0, NC):
                            t0, tn = CHUNKS[c]
                            pe.wait_ge(acc_freed[1 - s][c], j + s + START)
                            for k in range(KB):
                                for w, u in ((w_hi, ut_hi), (w_hi, ut_lo), (w_lo, ut_hi)):
                                    last = nc.tensor.matmul(acc[c][:, 0:tn], w[s][:, k, :], u[:, k, t0:t0 + tn],
                                                            start=(k == 0 and u is ut_hi and w is w_hi),
                                                            stop=(k == KB - 1 and w is w_lo))
                            last.then_inc(acc_ready[s][c], 1)

        @block.scalar
        def _(act):
            for kind, b0, n, c0, outs in KINDS:
                with act.Fori(0, n // 2) as i:
                    for s in range(2):
                        j = i + b0 // 2
                        if kind == "conv":
                            act.dma_start(taps[s][:, :], conv_wb[bass.ds(i * 2 + s, 1), :, :]
                                          .rearrange("b p k -> (b p) k")).then_inc(taps_loaded[s], 16)
                            act.wait_ge(conv_step[s], (i + 1) * CONV + START)
                            nc.scalar.activation(row_a[s][:, LEAD:LEAD + T], row_b[s][:, LEAD:LEAD + T],
                                                 ACT.Silu).then_inc(silu_done[s], 1)
                            continue
                        act.wait_ge(stored[s], (i * len(outs) + stores_before(kind)) * 16 + START)
                        for c in range(c0, NC):
                            t0, tn = CHUNKS[c]
                            to = row_a[s][:, LEAD + t0:LEAD + t0 + tn]
                            act.wait_ge(acc_ready[s][c], j + 1 + START)
                            if kind == "gate":
                                nc.scalar.activation(to, acc[c][:, 0:tn], ACT.Silu).then_inc(acc_freed[s][c], 1)
                            else:
                                nc.scalar.activation(to.bitcast(F32R), acc[c][:, 0:tn], ACT.Copy,
                                                     scale=Q_SCALE if kind == "q" else 1.0).then_inc(acc_high[s][c], 1)

        @block.vector
        def _(dve):
            highs = 0
            for kind, b0, n, c0, outs in KINDS:
                if kind == "gate":
                    continue
                with dve.Fori(0, n // 2) as i:
                    for s in range(2):
                        j = i + b0 // 2
                        if kind == "conv":
                            dve.wait_ge(stored[s], (i * len(outs) + stores_before(kind)) * 16 + START)
                        for c in range(c0, NC):
                            t0, tn = CHUNKS[c]
                            cols = slice(LEAD + t0, LEAD + t0 + tn)
                            if kind == "conv":
                                dve.wait_ge(acc_ready[s][c], j + 1 + START)
                                nc.vector.tensor_copy(row_a[s][:, cols], acc[c][:, 0:tn]).then_inc(acc_freed[s][c], 1)
                            else:
                                dve.wait_ge(acc_high[s][c], i + (highs + 1) + START)
                                nc.vector.scalar_tensor_tensor(
                                    out=row_b[s][:, cols].bitcast(F32R), in0=acc[c][:, 0:tn],
                                    scalar=Q_SCALE if kind == "q" else 1.0, in1=row_a[s][:, cols],
                                    op0=ALU.mult, op1=ALU.subtract).then_inc(acc_freed[s][c], 1)
                        if kind == "conv":
                            dve.wait_ge(acc_freed[s][LAST], j + 1 + START)
                            dve.wait_ge(lead_zero, START + 2)
                            dve.wait_ge(taps_loaded[s], i * 16 + 16 + START)
                            out = row_b[s][:, LEAD:LEAD + T]
                            for tap in range(CONV):
                                shifted = row_a[s][:, 1 + tap:1 + tap + T]
                                if tap == 0:
                                    done = nc.vector.tensor_scalar(out, shifted, taps[s][:, 0:1],
                                                                   taps[s][:, CONV:CONV + 1], ALU.mult, ALU.add)
                                else:
                                    dve.wait_ge(conv_step[s], i * CONV + tap + START)
                                    done = nc.vector.scalar_tensor_tensor(
                                        out=out, in0=shifted, scalar=taps[s][:, tap:tap + 1], in1=out,
                                        op0=ALU.mult, op1=ALU.add)
                                done.then_inc(conv_step[s], 1)
                if kind == "k":
                    highs = n // 2


def token_stage(nc, w_blocks, w_dt, dt_cols, ut_hi, ut_lo, dt_tok, scratch):
    with ExitStack() as ctx:
        m = Memory(nc, ctx)
        RING = 4
        CB = W // P
        stage = m.sbuf("t_stage", [P, CB, KB, P])
        w_hi = m.sbuf("t_w_hi", [P, CB, KB, P], F32R)
        w_lo = m.sbuf("t_w_lo", [P, CB, KB, P], F32R)
        out = [m.sbuf(f"t_out{r}", [P, W]) for r in range(RING + 1)]
        wd = m.sbuf("t_wd", [P, KB, HEADS])
        wd_hi = m.sbuf("t_wd_hi", [P, KB, HEADS], F32R)
        wd_lo = m.sbuf("t_wd_lo", [P, KB, HEADS], F32R)
        dtc = m.sbuf("t_dtc", [HEADS, 2])
        rate = m.sbuf("t_rate", [HEADS, 2])
        ident = m.sbuf("t_ident", [HEADS, HEADS])
        dx, da = m.sbuf("t_dx", [HEADS, W]), m.sbuf("t_da", [HEADS, W])
        de, dl = m.sbuf("t_de", [HEADS, W]), m.sbuf("t_dl", [HEADS, W])
        dt_row, dta_row = m.sbuf("t_dt_row", [HEADS, W]), m.sbuf("t_dta_row", [HEADS, W])
        dacc = m.psum("t_dacc", [P, W])
        dtp = m.psum("t_dtp", [P, CB, 2, HEADS])
        acc = [m.psum(f"t_acc{r}", [P, W]) for r in range(RING + 1)]
        small_loaded, w_loaded = m.sem("t_small_loaded"), m.sem("t_w_loaded")
        ident_zero, ident_ready = m.sem("t_ident_zero"), m.sem("t_ident_ready")
        wd_split, rate_step = m.sem("wd_split"), m.sem("rate_step")
        w_high, w_low = m.sem("t_w_high"), m.sem("t_w_low")
        acc_ready = m.sems("t_acc_ready", RING + 1)
        acc_freed = m.sems("t_acc_freed", RING + 1)
        stored = m.sems("t_stored", RING + 1)
        dacc_ready, dx_ready, da_ready = m.sem("dacc_ready"), m.sem("dx_ready"), m.sem("da_ready")
        de_ready, dl_ready, dt_ready, dta_ready = m.sem("de_ready"), m.sem("dl_ready"), m.sem("dt_ready"), m.sem("dta_ready")
        dt_turned, dt_kept = m.sem("dt_turned"), m.sem("dt_kept")
        m.start()
        block = ctx.enter_context(nc.Block())

        PER = NT // RING
        KINDS = [("v", V_BLOCK, True)]
        NCH = D // W

        @block.sync
        def _(sp):
            sp.dma_start(wd[:, :, :], w_dt).then_inc(small_loaded, 16)
            sp.dma_start(dtc[:, :], dt_cols).then_inc(small_loaded, 16)
            for n, (kind, b0, with_meta) in enumerate(KINDS):
                with sp.Fori(0, NCH) as i:
                    done = i + n * NCH
                    sp.wait_ge(w_high, done * CB + START)
                    sp.wait_ge(w_low, done * CB + START)
                    sp.dma_start(stage[:, :, :, :], w_blocks[bass.ds(i * CB + b0, CB), :, :, :]
                                 .rearrange("b p k c -> p b k c")).then_inc(w_loaded, 16)
                    if with_meta:
                        sp.wait_ge(acc_freed[RING], i + 1 + START)
                        sp.dma_start(scratch["v"][0:META, bass.ds(i * W, W)],
                                     out[RING][0:META, :]).then_inc(stored[RING], 16)
                    for tile in range(NT):
                        r = tile % RING
                        sp.wait_ge(acc_freed[r], done * PER + (tile // RING + 1) + START)
                        row = META + tile * P if with_meta else tile * P
                        sp.dma_start(scratch[kind][row:row + P, bass.ds(i * W, W)],
                                     out[r][:, :]).then_inc(stored[r], 16)
            for r in range(RING):
                sp.wait_ge(stored[r], 16 * NCH * PER + START)
            sp.wait_ge(stored[RING], 16 * NCH + START)

        @block.gpsimd
        def _(pool):
            nc.gpsimd.memset(ident[:, :], 0.0).then_inc(ident_zero, 1)
            pool.wait_ge(ident_zero, START + 1)
            nc.gpsimd.affine_select(out=ident[:, :], in_=ident[:, :], compare_op=ALU.not_equal, fill=1.0,
                                    base=0, pattern=[[-1, HEADS]], channel_multiplier=1).then_inc(ident_ready, 1)
            pool.wait_ge(small_loaded, START + 32)
            nc.gpsimd.tensor_copy(wd_hi[:, :, :], wd[:, :, :]).then_inc(wd_split, 1)
            pool.wait_ge(wd_split, START + 1)
            nc.gpsimd.tensor_tensor(wd_lo[:, :, :], wd[:, :, :], wd_hi[:, :, :].bitcast(F32),
                                    ALU.subtract).then_inc(wd_split, 1)

        @block.tensor
        def _(pe):
            pe.wait_ge(wd_split, START + 2)
            pe.wait_ge(ident_ready, START + 1)
            for c, (t0, tn) in enumerate(CHUNKS):
                if c:
                    pe.wait_ge(dx_ready, c + START)
                for k in range(KB):
                    for w, u in ((wd_hi, ut_hi), (wd_hi, ut_lo), (wd_lo, ut_hi)):
                        last = nc.tensor.matmul(dacc[0:HEADS, 0:tn], w[:, k, :], u[:, k, t0:t0 + tn],
                                                start=(k == 0 and u is ut_hi and w is wd_hi),
                                                stop=(k == KB - 1 and w is wd_lo))
                last.then_inc(dacc_ready, 1)
                pe.wait_ge(dta_ready, c + 1 + START)
                if c:
                    pe.wait_ge(dt_kept, c + START)
                tiles = max(tn // P, 1)
                rows = min(tn, P)
                for q in range(tiles):
                    for half, row in enumerate((dt_row, dta_row)):
                        last = nc.tensor.transpose(dtp[0:rows, q, half, :], row[:, q * P:q * P + rows], ident[:, :])
                last.then_inc(dt_turned, 1)
            for n, (kind, _, with_meta) in enumerate(KINDS):
                with pe.Fori(0, NCH) as i:
                    done = i + n * NCH
                    tiles = ([(RING, 0, META, i)] if with_meta else []) + [
                        (t % RING, META + t * P, P, done * PER + t // RING) for t in range(NT)]
                    for at, (r, t0, tn, uses) in enumerate(tiles):
                        if at == 0:
                            pe.wait_ge(w_high, done * CB + CB + START)
                            pe.wait_ge(w_low, done * CB + CB + START)
                        pe.wait_ge(acc_freed[r], uses + START)
                        for k in range(KB):
                            for u, w in ((ut_hi, w_hi), (ut_hi, w_lo), (ut_lo, w_hi)):
                                last = nc.tensor.matmul(acc[r][0:tn, :], u[:, k, t0:t0 + tn], w[:, :, k, :],
                                                        start=(k == 0 and u is ut_hi and w is w_hi),
                                                        stop=(k == KB - 1 and u is ut_lo))
                        last.then_inc(acc_ready[r], 1)

        def each_chunk(eng, take):
            for n, (kind, _, with_meta) in enumerate(KINDS):
                with eng.Fori(0, NCH) as i:
                    take(i + n * NCH, i, kind, with_meta)

        @block.scalar
        def _(act):
            act.wait_ge(small_loaded, START + 32)
            nc.scalar.activation(rate[:, 0:1], dtc[:, 1:2], ACT.Exp).then_inc(rate_step, 1)
            for c, (t0, tn) in enumerate(CHUNKS):
                act.wait_ge(dacc_ready, c + 1 + START)
                if c:
                    act.wait_ge(dt_ready, c + START)
                nc.scalar.activation(dx[:, 0:tn], dacc[0:HEADS, 0:tn], ACT.Identity,
                                     bias=dtc[:, 0:1]).then_inc(dx_ready, 1)
                act.wait_ge(da_ready, c + 1 + START)
                nc.scalar.activation(de[:, 0:tn], da[:, 0:tn], ACT.Exp).then_inc(de_ready, 1)
                act.wait_ge(de_ready, c + 1 + START)
                nc.scalar.activation(dl[:, 0:tn], de[:, 0:tn], ACT.Ln, bias=1.0).then_inc(dl_ready, 1)

            def take(done, i, kind, with_meta):
                act.wait_ge(w_loaded, done * 16 + 16 + START)
                if with_meta:
                    pass
                act.wait_ge(acc_ready[(NT - 1) % RING], done * PER + START)
                for b in range(CB):
                    nc.scalar.activation(w_hi[:, b, :, :], stage[:, b, :, :], ACT.Copy).then_inc(w_high, 1)
                if with_meta:
                    act.wait_ge(acc_ready[RING], i + 1 + START)
                    act.wait_ge(stored[RING], i * 16 + START)
                    nc.scalar.activation(out[RING][0:META, :], acc[RING][0:META, :],
                                         ACT.Copy).then_inc(acc_freed[RING], 1)
                for t in range(NT):
                    r = t % RING
                    act.wait_ge(acc_ready[r], done * PER + (t // RING + 1) + START)
                    act.wait_ge(stored[r], (done * PER + t // RING) * 16 + START)
                    nc.scalar.activation(out[r][:, :], acc[r][:, :],
                                         ACT.Silu if kind == "z" else ACT.Copy).then_inc(acc_freed[r], 1)

            each_chunk(act, take)

        @block.vector
        def _(dve):
            dve.wait_ge(rate_step, START + 1)
            nc.vector.tensor_scalar(rate[:, 1:2], rate[:, 0:1], -1.0, None, ALU.mult).then_inc(rate_step, 1)
            for c, (t0, tn) in enumerate(CHUNKS):
                dve.wait_ge(dx_ready, c + 1 + START)
                if c:
                    dve.wait_ge(de_ready, c + START)
                nc.vector.scalar_tensor_tensor(out=da[:, 0:tn], in0=dx[:, 0:tn], scalar=-1.0, in1=dx[:, 0:tn],
                                               op0=ALU.mult, op1=ALU.min).then_inc(da_ready, 1)
                dve.wait_ge(dl_ready, c + 1 + START)
                if c:
                    dve.wait_ge(dt_turned, c + START)
                nc.vector.scalar_tensor_tensor(out=dt_row[:, 0:tn], in0=dx[:, 0:tn], scalar=0.0, in1=dl[:, 0:tn],
                                               op0=ALU.max, op1=ALU.add).then_inc(dt_ready, 1)
                dve.wait_ge(dt_ready, c + 1 + START)
                dve.wait_ge(rate_step, START + 2)
                nc.vector.tensor_scalar(dta_row[:, 0:tn], dt_row[:, 0:tn], rate[:, 1:2], None,
                                        ALU.mult).then_inc(dta_ready, 1)
                dve.wait_ge(dt_turned, c + 1 + START)
                if c == 0:
                    nc.vector.tensor_copy(dt_tok[0:META, 0, :, :], dtp[0:META, 0, :, :]).then_inc(dt_kept, 1)
                else:
                    q0 = 1 + (c - 1) * CB
                    nc.vector.tensor_copy(dt_tok[:, q0:q0 + CB, :, :], dtp[:, :, :, :]).then_inc(dt_kept, 1)

            def take(done, i, kind, with_meta):
                dve.wait_ge(acc_ready[(NT - 1) % RING], done * PER + START)
                for b in range(CB):
                    dve.wait_ge(w_high, done * CB + (b + 1) + START)
                    nc.vector.tensor_tensor(w_lo[:, b, :, :], stage[:, b, :, :], w_hi[:, b, :, :].bitcast(F32),
                                            ALU.subtract).then_inc(w_low, 1)

            each_chunk(dve, take)


def over_heads(columns, n):
    return columns.unsqueeze(2).to_broadcast([columns.shape[0], columns.shape[1], n])


def triangles(nc, pool, upper, later, zeroed, ready):
    for tile in (upper, later):
        nc.gpsimd.memset(tile[:, :], 1.0).then_inc(zeroed, 1)
    pool.wait_ge(zeroed, START + 2)
    nc.gpsimd.affine_select(out=upper[:, :], in_=upper[:, :], compare_op=ALU.is_ge, fill=0.0, base=0,
                            pattern=[[1, P]], channel_multiplier=-1).then_inc(ready, 1)
    nc.gpsimd.affine_select(out=later[:, :], in_=later[:, :], compare_op=ALU.is_gt, fill=0.0, base=0,
                            pattern=[[-1, P]], channel_multiplier=1).then_inc(ready, 1)


def scan_start(nc, scratch, dt_tok, state):
    with ExitStack() as ctx:
        m = Memory(nc, ctx)
        xc = m.sbuf("s0_xc", [P, KB + GROUPS, META])
        ident = m.sbuf("s0_ident", [P, P])
        ones, later = m.sbuf("s0_ones", [META, META]), m.sbuf("s0_later", [META, META])
        b_tok = m.sbuf("s0_b", [META, GROUPS, STATE])
        decay = m.sbuf("s0_decay", [META, HEADS])
        xdt, xde = m.sbuf("s0_xdt", [META, D]), m.sbuf("s0_xde", [META, D])
        px = m.psum("s0_px", [META, KB, P])
        pb = m.psum("s0_pb", [META, GROUPS, P])
        pd = m.psum("s0_pd", [META, HEADS])
        ps = m.psum("s0_ps", [P, GROUPS, W])
        loaded, made, ready = m.sem("s0_loaded"), m.sem("s0_made"), m.sem("s0_ready")
        turned, decay_ready, b_ready, xdt_ready, xde_ready = (m.sem(f"s0_{n}") for n in (
            "turned", "decay_ready", "b_ready", "xdt_ready", "xde_ready"))
        summed, state_ready = m.sem("s0_summed"), m.sem("s0_state_ready")
        m.start()
        block = ctx.enter_context(nc.Block())

        @block.sync
        def _(sp):
            sp.dma_start(xc[:, :, :], scratch["xbc"][0:KB + GROUPS, :, 0:META]
                         .rearrange("b p t -> p b t")).then_inc(loaded, 16)

        @block.gpsimd
        def _(pool):
            nc.gpsimd.memset(ident[:, :], 0.0).then_inc(made, 1)
            nc.gpsimd.memset(ones[:, :], 1.0).then_inc(made, 1)
            pool.wait_ge(made, START + 2)
            nc.gpsimd.affine_select(out=ident[:, :], in_=ident[:, :], compare_op=ALU.not_equal, fill=1.0,
                                    base=0, pattern=[[-1, P]], channel_multiplier=1).then_inc(ready, 1)
            nc.gpsimd.affine_select(out=later[:, :], in_=ones[:, :], compare_op=ALU.is_gt, fill=0.0, base=0,
                                    pattern=[[-1, META]], channel_multiplier=1).then_inc(ready, 1)

        @block.tensor
        def _(pe):
            pe.wait_ge(ready, START + 2)
            pe.wait_ge(loaded, START + 16)
            for b in range(KB):
                nc.tensor.transpose(px[:, b, :], xc[:, b, :], ident[:, :])
            for g in range(GROUPS):
                nc.tensor.transpose(pb[:, g, :], xc[:, KB + g, :], ident[:, :])
            nc.tensor.matmul(pd[:, :], later[:, :], dt_tok[0:META, 0, 1, :], start=True, stop=True).then_inc(turned, 1)
            pe.wait_ge(b_ready, START + 1)
            pe.wait_ge(xde_ready, START + 1)
            for g in range(GROUPS):
                last = nc.tensor.matmul(ps[:, g, :], b_tok[:, g, :], xde[:, g * W:(g + 1) * W], start=True, stop=True)
            last.then_inc(summed, 1)

        @block.scalar
        def _(act):
            act.wait_ge(turned, START + 1)
            nc.scalar.activation(decay[:, :], pd[:, :], ACT.Exp).then_inc(decay_ready, 1)
            nc.scalar.activation(b_tok[:, :, :], pb[:, :, :], ACT.Copy).then_inc(b_ready, 1)

        @block.vector
        def _(dve):
            dve.wait_ge(turned, START + 1)
            nc.vector.tensor_tensor(xdt[:, :].rearrange("p (h c) -> p h c", h=HEADS),
                                    px[:, :, :].rearrange("p b (h c) -> p (b h) c", h=2),
                                    over_heads(dt_tok[0:META, 0, 0, :], HEAD), ALU.mult).then_inc(xdt_ready, 1)
            dve.wait_ge(xdt_ready, START + 1)
            dve.wait_ge(decay_ready, START + 1)
            nc.vector.tensor_tensor(xde[:, :].rearrange("p (h c) -> p h c", h=HEADS),
                                    xdt[:, :].rearrange("p (h c) -> p h c", h=HEADS),
                                    over_heads(decay[:, :], HEAD), ALU.mult).then_inc(xde_ready, 1)
            dve.wait_ge(summed, START + 1)
            nc.vector.tensor_copy(state[:, :, :], ps[:, :, :]).then_inc(state_ready, 1)


def scan_stage(nc, scratch, d_cols, dt_tok, state):
    with ExitStack() as ctx:
        m = Memory(nc, ctx)
        GB = KB // GROUPS
        upper, later, ones = m.sbuf("s_upper", [P, P]), m.sbuf("s_later", [P, P]), m.sbuf("s_ones", [P, P])
        ident = m.sbuf("s_ident", [P, P])
        d_col = m.sbuf("s_d_col", [P, KB])
        xc = [m.sbuf(f"s_xc{s}", [P, XB, P]) for s in range(2)]
        zt = [m.sbuf(f"s_zt{s}", [P, KB, P]) for s in range(2)]
        b_tok = [m.sbuf(f"s_b{s}", [P, GROUPS, STATE]) for s in range(2)]
        expo = [m.sbuf(f"s_expo{s}", [P, 3, HEADS]) for s in range(2)]
        cbm = [m.sbuf(f"s_cbm{s}", [P, GROUPS, P]) for s in range(2)]
        ua = [m.sbuf(f"s_ua{g}", [P, HPG, P]) for g in range(GROUPS)]
        decay = [m.sbuf(f"s_decay{g}", [P, HPG, P]) for g in range(GROUPS)]
        mt = [m.sbuf(f"s_mt{g}", [P, HPG, P]) for g in range(GROUPS)]
        xdt = [m.sbuf(f"s_xdt{g}", [P, W]) for g in range(GROUPS)]
        xde = [m.sbuf(f"s_xde{g}", [P, W]) for g in range(GROUPS)]
        yo = [m.sbuf(f"s_yo{g}", [P, W]) for g in range(GROUPS)]
        ysum = [m.sbuf(f"s_ysum{g}", [P, W]) for g in range(GROUPS)]
        xd = [m.sbuf(f"s_xd{g}", [P, GB, P]) for g in range(GROUPS)]
        yt = [m.sbuf(f"s_yt{g}", [P, GB, P]) for g in range(GROUPS)]
        gated = [m.sbuf(f"s_gated{g}", [P, GB, P]) for g in range(GROUPS)]
        px = m.psum("s_px", [P, GB, P])
        pbc = m.psum("s_pbc", [P, 2 * GROUPS, P])
        pc = m.psum("s_pc", [P, 3, HEADS])
        pseg = m.psum("s_pseg", [P, HPG, P])
        pyo, pyd, pst = m.psum("s_pyo", [P, W]), m.psum("s_pyd", [P, W]), m.psum("s_pst", [P, W])

        def per_unit(name):
            return [m.sems(f"{name}{s}", GROUPS) for s in range(2)]

        d_loaded, filled, made = m.sem("d_loaded"), m.sem("s_filled"), m.sem("s_made")
        xc_loaded, zt_loaded = m.sems("xc_loaded", 2), m.sems("zt_loaded", 2)
        bc_ready, sums_ready = m.sems("bc_ready", 2), m.sems("sums_ready", 2)
        b_ready, expo_ready, cbm_ready = m.sems("b_ready", 2), m.sems("expo_ready", 2), m.sems("cbm_ready", 2)
        x_turned, ua_ready, seg_ready, decay_ready = (per_unit(n) for n in ("x_turned", "ua_ready", "seg_ready", "decay_ready"))
        xdt_ready, xde_ready, m_ready = (per_unit(n) for n in ("xdt_ready", "xde_ready", "m_ready"))
        off_done, st_done, diag_done = (per_unit(n) for n in ("off_done", "st_done", "diag_done"))
        yo_ready, decayed, state_ready, ysum_ready = (per_unit(n) for n in ("yo_ready", "decayed", "state_ready", "ysum_ready"))
        y_turned, xd_ready, yt_ready, gated_ready = (per_unit(n) for n in ("y_turned", "xd_ready", "yt_ready", "gated_ready"))
        stored = m.sems("s_stored", GROUPS)
        m.start()
        block = ctx.enter_context(nc.Block())
        PAIRS_OF_CHUNKS = NT // 2

        def before(s, g, i):
            return (s, 0, i + 1) if g else (1 - s, 1, i + s)

        def dt_of(i, s, which, g):
            if isinstance(i, int):
                return dt_tok[:, 1 + 2 * i + s, which, g * HPG:(g + 1) * HPG]
            return dt_tok[:, bass.ds(i * 2 + (1 + s), 1), which, g * HPG:(g + 1) * HPG].rearrange("p o h -> p (o h)")

        def pipeline(eng, *stages):
            EACH = 2 * GROUPS
            LAST = PAIRS_OF_CHUNKS - 1

            def step(i, j):
                for ahead, do in stages:
                    shift, unit = (j + ahead) // EACH, (j + ahead) % EACH
                    at = i + shift if shift else i
                    if not isinstance(at, int) or 0 <= at <= LAST:
                        do(unit // GROUPS, unit % GROUPS, at)

            for j in range(-2, EACH):
                step(0, j)
            with eng.Fori(1, LAST) as i:
                for j in range(EACH):
                    step(i, j)
            for j in range(EACH + 1):
                step(LAST, j)

        @block.sync
        def _(sp):
            sp.dma_start(d_col[:, :], d_cols).then_inc(d_loaded, 16)

            def load_xc(s, i):
                sp.dma_start(xc[s][:, :, :], scratch["xbc"][:, :, bass.ds(i * (2 * P) + (s * P + META), P)]
                             .rearrange("b p t -> p b t")).then_inc(xc_loaded[s], 16)

            def load_zt(s, i):
                sp.dma_start(zt[s][:, :, :], scratch["gate"][KB:MB, :, bass.ds(i * (2 * P) + s * P, P)]
                             .rearrange("b p t -> p b t")).then_inc(zt_loaded[s], 16)

            def store(s, g, i):
                sp.wait_ge(gated_ready[s][g], i + 1 + START)
                sp.dma_start(scratch["mixed"][KB + g * GB:KB + (g + 1) * GB, :, bass.ds(i * (2 * P) + s * P, P)]
                             .rearrange("b p t -> p b t"), gated[g][:, :, :]).then_inc(stored[g], 16)

            def step(i, more):
                for s in range(2):
                    store(s, 0, i)
                    if more:
                        sp.wait_ge(off_done[s][1], i + 1 + START)
                        sp.wait_ge(xd_ready[s][1], i + 1 + START)
                        load_xc(s, i + 1)
                    store(s, 1, i)
                    if more:
                        load_zt(s, i + 1)

            for s in range(2):
                load_xc(s, 0)
            for s in range(2):
                load_zt(s, 0)
            with sp.Fori(0, PAIRS_OF_CHUNKS - 1) as i:
                step(i, True)
            step(PAIRS_OF_CHUNKS - 1, False)
            for g in range(GROUPS):
                sp.wait_ge(stored[g], 16 * NT + START)

        @block.gpsimd
        def _(pool):
            triangles(nc, pool, upper, later, filled, made)
            nc.gpsimd.memset(ones[:, :], 1.0).then_inc(made, 1)
            nc.gpsimd.memset(ident[:, :], 0.0).then_inc(filled, 1)
            pool.wait_ge(filled, START + 3)
            nc.gpsimd.affine_select(out=ident[:, :], in_=ident[:, :], compare_op=ALU.not_equal, fill=1.0,
                                    base=0, pattern=[[-1, P]], channel_multiplier=1).then_inc(made, 1)
            pool.wait_ge(made, START + 4)
            pool.wait_ge(d_loaded, START + 16)

            def spread_steps(s, g, i):
                pool.wait_ge(seg_ready[1 - s][g], i + s + START)
                nc.gpsimd.tensor_tensor(ua[g][:, :, :], upper[:, :].unsqueeze(1).to_broadcast([P, HPG, P]),
                                        over_heads(dt_of(i, s, 1, g), P), ALU.mult).then_inc(ua_ready[s][g], 1)

            def skip(s, g, i):
                pool.wait_ge(xc_loaded[s], i * 16 + 16 + START)
                pool.wait_ge(yt_ready[1 - s][g], i + s + START)
                nc.gpsimd.tensor_tensor(xd[g][:, :, :], xc[s][:, g * GB:(g + 1) * GB, :],
                                        spread(d_col[:, g * GB:(g + 1) * GB], P), ALU.mult).then_inc(xd_ready[s][g], 1)

            def gate(s, g, i):
                pool.wait_ge(zt_loaded[s], i * 16 + 16 + START)
                pool.wait_ge(yt_ready[s][g], i + 1 + START)
                pool.wait_ge(stored[g], i * 32 + 16 * s + START)
                nc.gpsimd.tensor_tensor(gated[g][:, :, :], yt[g][:, :, :], zt[s][:, g * GB:(g + 1) * GB, :],
                                        ALU.mult).then_inc(gated_ready[s][g], 1)

            pipeline(pool, (2, spread_steps), (1, skip), (-1, gate))

        @block.tensor
        def _(pe):
            pe.wait_ge(made, START + 4)

            def front(s, g, i):
                if g == 0:
                    pe.wait_ge(xc_loaded[s], i * 16 + 16 + START)
                    pe.wait_ge(b_ready[1 - s], i + s + START)
                    pe.wait_ge(cbm_ready[1 - s], i + s + START)
                    for q in range(GROUPS):
                        nc.tensor.transpose(pbc[:, q, :], xc[s][:, KB + q, :], ident[:, :])
                    for q in range(GROUPS):
                        last = nc.tensor.matmul(pbc[:, GROUPS + q, :], xc[s][:, KB + q, :], xc[s][:, KB + GROUPS + q, :],
                                                start=True, stop=True)
                    last.then_inc(bc_ready[s], 1)
                    pe.wait_ge(expo_ready[1 - s], i + s + START)
                    for n, lhs in enumerate((upper, later, ones)):
                        rhs = (dt_tok[:, 1 + 2 * i + s, 1, :] if isinstance(i, int) else
                               dt_tok[:, bass.ds(i * 2 + (1 + s), 1), 1, :].rearrange("p o h -> p (o h)"))
                        last = nc.tensor.matmul(pc[:, n, :], lhs[:, :], rhs, start=True, stop=True)
                    last.then_inc(sums_ready[s], 1)
                ps, pg, count = before(s, g, i)
                pe.wait_ge(xdt_ready[ps][pg], count + START)
                for b in range(GB):
                    last = nc.tensor.transpose(px[:, b, :], xc[s][:, g * GB + b, :], ident[:, :])
                last.then_inc(x_turned[s][g], 1)
                pe.wait_ge(ua_ready[s][g], i + 1 + START)
                pe.wait_ge(decay_ready[ps][pg], count + START)
                for half in range(2):
                    hs = slice(half * (HPG // 2), (half + 1) * (HPG // 2))
                    last = nc.tensor.matmul(pseg[:, hs, :], later[:, :], ua[g][:, hs, :], start=True, stop=True)
                last.then_inc(seg_ready[s][g], 1)

            def turn(s, g, i):
                pe.wait_ge(ysum_ready[s][g], i + 1 + START)
                for b in range(GB):
                    last = nc.tensor.transpose(pyd[:, b * P:(b + 1) * P], ysum[g][:, b * P:(b + 1) * P], ident[:, :])
                last.then_inc(y_turned[s][g], 1)

            def multiply(s, g, i):
                ps, pg, count = before(s, g, i)
                pe.wait_ge(state_ready[1 - s][g], i + s + START)
                pe.wait_ge(yo_ready[ps][pg], count + START)
                nc.tensor.matmul(pyo[:, :], xc[s][:, KB + GROUPS + g, :], state[:, g, :],
                                 start=True, stop=True).then_inc(off_done[s][g], 1)
                pe.wait_ge(b_ready[s], i + 1 + START)
                pe.wait_ge(xde_ready[s][g], i + 1 + START)
                pe.wait_ge(state_ready[ps][pg], count + START)
                nc.tensor.matmul(pst[:, :], b_tok[s][:, g, :], xde[g][:, :], start=True, stop=True).then_inc(st_done[s][g], 1)
                pe.wait_ge(m_ready[s][g], i + 1 + START)
                pe.wait_ge(yt_ready[ps][pg], count + START)
                for h in range(HPG):
                    last = nc.tensor.matmul(pyd[:, h * HEAD:(h + 1) * HEAD], mt[g][:, h, :],
                                            xdt[g][:, h * HEAD:(h + 1) * HEAD], start=True, stop=True)
                last.then_inc(diag_done[s][g], 1)

            pipeline(pe, (1, front), (-1, turn), (0, multiply))

        @block.scalar
        def _(act):
            def front(s, g, i):
                if g == 0:
                    act.wait_ge(bc_ready[s], i + 1 + START)
                    act.wait_ge(st_done[s][1], i + START)
                    nc.scalar.activation(b_tok[s][:, :, :], pbc[:, 0:GROUPS, :], ACT.Copy).then_inc(b_ready[s], 1)
                    act.wait_ge(sums_ready[s], i + 1 + START)
                    act.wait_ge(decayed[s][1], i + START)
                    nc.scalar.activation(expo[s][:, :, :], pc[:, :, :], ACT.Exp).then_inc(expo_ready[s], 1)
                act.wait_ge(seg_ready[s][g], i + 1 + START)
                act.wait_ge(m_ready[1 - s][g], i + s + START)
                nc.scalar.activation(decay[g][:, :, :], pseg[:, :, :], ACT.Exp).then_inc(decay_ready[s][g], 1)

            pipeline(act, (1, front))

        @block.vector
        def _(dve):
            dve.wait_ge(made, START + 4)

            def heads(tile):
                return tile[:, :].rearrange("p (h c) -> p h c", h=HPG)

            def inputs(s, g, i):
                hs = slice(g * HPG, (g + 1) * HPG)
                if g == 0:
                    dve.wait_ge(bc_ready[s], i + 1 + START)
                    dve.wait_ge(b_ready[s], i + 1 + START)
                    nc.vector.tensor_tensor(cbm[s][:, :, :], pbc[:, GROUPS:2 * GROUPS, :],
                                            upper[:, :].unsqueeze(1).to_broadcast([P, GROUPS, P]),
                                            ALU.mult).then_inc(cbm_ready[s], 1)
                dve.wait_ge(x_turned[s][g], i + 1 + START)
                dve.wait_ge(diag_done[1 - s][g], i + s + START)
                nc.vector.tensor_tensor(heads(xdt[g]), px[:, :, :].rearrange("p b (h c) -> p (b h) c", h=2),
                                        over_heads(dt_of(i, s, 0, g), HEAD), ALU.mult).then_inc(xdt_ready[s][g], 1)
                dve.wait_ge(xdt_ready[s][g], i + 1 + START)
                dve.wait_ge(expo_ready[s], i + 1 + START)
                dve.wait_ge(st_done[1 - s][g], i + s + START)
                nc.vector.tensor_tensor(heads(xde[g]), heads(xdt[g]), over_heads(expo[s][:, 1, hs], HEAD),
                                        ALU.mult).then_inc(xde_ready[s][g], 1)

            def weights(s, g, i):
                dve.wait_ge(decay_ready[s][g], i + 1 + START)
                dve.wait_ge(cbm_ready[s], i + 1 + START)
                nc.vector.tensor_tensor(mt[g][:, :, :], decay[g][:, :, :],
                                        cbm[s][:, g, :].unsqueeze(1).to_broadcast([P, HPG, P]),
                                        ALU.mult).then_inc(m_ready[s][g], 1)

            def states(s, g, i):
                hs = slice(g * HPG, (g + 1) * HPG)
                dve.wait_ge(off_done[s][g], i + 1 + START)
                nc.vector.tensor_tensor(heads(yo[g]), heads(pyo), over_heads(expo[s][:, 0, hs], HEAD),
                                        ALU.mult).then_inc(yo_ready[s][g], 1)
                own = state[:, g, :].rearrange("p (h c) -> p h c", h=HPG)
                nc.vector.tensor_tensor(own, own, over_heads(expo[s][:, 2, hs], HEAD), ALU.mult).then_inc(decayed[s][g], 1)
                dve.wait_ge(decayed[s][g], i + 1 + START)
                dve.wait_ge(st_done[s][g], i + 1 + START)
                nc.vector.tensor_tensor(state[:, g, :], state[:, g, :], pst[:, :], ALU.add).then_inc(state_ready[s][g], 1)

            def sum_y(s, g, i):
                dve.wait_ge(diag_done[s][g], i + 1 + START)
                dve.wait_ge(yo_ready[s][g], i + 1 + START)
                dve.wait_ge(y_turned[1 - s][g], i + s + START)
                nc.vector.tensor_tensor(ysum[g][:, :], yo[g][:, :], pyd[:, :], ALU.add).then_inc(ysum_ready[s][g], 1)

            def add_skip(s, g, i):
                dve.wait_ge(y_turned[s][g], i + 1 + START)
                dve.wait_ge(xd_ready[s][g], i + 1 + START)
                dve.wait_ge(gated_ready[1 - s][g], i + s + START)
                nc.vector.tensor_tensor(yt[g][:, :, :], xd[g][:, :, :], pyd[:, :].rearrange("p (b c) -> p b c", b=GB),
                                        ALU.add).then_inc(yt_ready[s][g], 1)

            pipeline(dve, (1, inputs), (-1, add_skip), (0, states), (1, weights), (0, sum_y))


def key_block(kb):
    return (0, META) if kb == 0 else (META + (kb - 1) * P, P)


def attention_units():
    units = []
    for c in range(NW):
        prev = None
        for kb in range((c + 1) * (W // P), -1, -1):
            start = max(kb - 1 - c * (W // P), 0) * P if kb else 0
            units.append((c, kb, start, prev))
            prev = start
    return units


def attention_stage(nc, scratch):
    UNITS = attention_units()
    U = len(UNITS)
    N = 2 * U
    C = 2 * NW
    ITER = PAIRS // 2
    RING = 3
    FIRST = META + W

    def unit(n):
        return UNITS[n % U]

    def diagonal(n):
        c, kb, _, _ = unit(n)
        return kb > c * (W // P)

    def first(n):
        return unit(n)[3] is None

    def last(n):
        return unit(n)[1] == 0

    def rows(n):
        return key_block(unit(n)[1])[1]

    def bank(n):
        return n % N % RING

    def bank_before(n):
        return next(x for x in range(n - 1, n - 2 * RING, -1) if bank(x % N) == bank(n))

    def having(test, n):
        return sum(test(x) for x in range(n)) if n >= 0 else -sum(test(x % N) for x in range(n, 0))

    def carried(n):
        return not first(n)

    def chunk_of(n):
        return n // U * NW + unit(n)[0]

    CARRIED = having(carried, N)

    with ExitStack() as ctx:
        m = Memory(nc, ctx)

        def ring(name, n, dt=F32, shape=(P, 2, W)):
            return [m.sbuf(f"a_{name}{r}", list(shape), dt) for r in range(n)]

        k_high, k_low = ring("k_high", 2, F32R, (P, 2, T)), ring("k_low", 2, F32R, (P, 2, T))
        v = ring("v", 2, F32, (P, NT + 1, P))
        q = ring("q", 2, F32R)
        gate = ring("gate", 2, F32, (P, W))
        out = ring("out", 2, F32, (P, W))
        soft = ring("soft", RING)
        sp_ = ring("sp", RING)
        sp_hi, sp_lo = ring("sp_hi", RING, F32R), ring("sp_lo", RING, F32R)
        newer = ring("newer", RING)
        w = ring("w", RING)
        plain = m.sbuf("a_plain", [P, 2, P])
        minus = m.sbuf("a_minus", [P, P], F32R)
        ident = m.sbuf("a_ident", [P, P], BF16)
        never = m.sbuf("a_never", [P, P], BF16)
        zero = m.sbuf("a_zero", [P, 1])
        z = [m.psum(f"a_z{r}", [P, 2, W]) for r in range(RING)]
        o = [m.psum(f"a_o{r}", [P, W]) for r in range(2)]

        filled, made, minus_ready = m.sem("a_filled"), m.sem("a_made"), m.sem("minus_ready")
        k_loaded = [m.sems(f"k_loaded{slot}", 2) for slot in range(2)]
        v_loaded = [m.sems(f"v_loaded{slot}", 2) for slot in range(2)]
        q_loaded, gate_loaded = m.sems("q_loaded", 2), m.sems("gate_loaded", 2)
        stored = m.sems("a_stored", 2)
        COUNTERS = ("z_ready", "exp_ready", "capped", "ln_ready", "sp_ready", "high_ready", "low_ready", "newer_ready",
                    "summed_0", "summed", "w_0_ready", "w_ready", "applied", "out_ready")
        count = {name: m.sem(name) for name in COUNTERS}

        m.start()
        block = ctx.enter_context(nc.Block())

        def await_units(eng, name, it, n, total=N):
            eng.wait_ge(count[name], it * total + (n + START))

        def done(name, instruction):
            instruction.then_inc(count[name], 1)

        def columns(tile, n, lo=None, hi=W):
            return tile[0:rows(n), :, (unit(n)[2] if lo is None else lo):hi]

        @block.sync
        def _(sp):
            def load_pair(slot, it, part):
                pair = it * 2 + slot
                one = lambda name: scratch[name][bass.ds(pair, 1), :, :].rearrange("b (h p) t -> p (b h) t", h=2)
                if part == 0:
                    sp.dma_start(v[slot][0:META, 0, :],
                                 scratch["v"][0:META, bass.ds(pair * P, P)]).then_inc(v_loaded[slot][0], 16)
                t0, t1 = ((0, FIRST), (FIRST, T))[part]
                b0, b1 = 1 + max(t0 - META, 0) // P, 1 + (t1 - META) // P
                for tile, name in ((k_high, "k_hi"), (k_low, "k_lo")):
                    for half in range(2):
                        sp.dma_start(tile[slot][half * HEAD:(half + 1) * HEAD, :, t0:t1].bitcast(F32),
                                     one(name)[:, :, t0:t1]).then_inc(k_loaded[slot][part], 16)
                sp.dma_start(v[slot][:, b0:b1, :], scratch["v"][META + (b0 - 1) * P:t1, bass.ds(pair * P, P)]
                             .rearrange("(b p) c -> p b c", p=P)).then_inc(v_loaded[slot][part], 16)

            def load_chunk(ch, it):
                pair, c, r = it * 2 + ch // NW, ch % NW, ch % 2
                for half, name in enumerate(("q_hi", "q_lo")):
                    sp.dma_start(q[r][half * HEAD:(half + 1) * HEAD, :, :].bitcast(F32),
                                 scratch[name][bass.ds(pair, 1), :, c * W:(c + 1) * W]
                                 .rearrange("b (h p) t -> p (b h) t", h=2)).then_inc(q_loaded[r], 16)
                sp.dma_start(gate[r][:, :], scratch["gate"][bass.ds(pair, 1), :, c * W:(c + 1) * W]
                             .rearrange("b p t -> (b p) t")).then_inc(gate_loaded[r], 16)

            def step(it, more):
                for ch in range(C):
                    await_units(sp, "out_ready", it, ch + 1, C)
                    sp.dma_start(scratch["mixed"][bass.ds(it * 2 + ch // NW, 1), :, ch % NW * W:(ch % NW + 1) * W]
                                 .rearrange("b p t -> (b p) t"), out[ch % 2][:, :]).then_inc(stored[ch % 2], 16)
                    if ch + 2 < C:
                        load_chunk(ch + 2, it)
                    elif more:
                        load_chunk(ch + 2 - C, it + 1)
                    if ch % NW == NW - 1 and more:
                        for part in range(2):
                            load_pair(ch // NW, it + 1, part)

            load_chunk(0, 0)
            load_pair(0, 0, 0)
            load_chunk(1, 0)
            load_pair(0, 0, 1)
            for part in range(2):
                load_pair(1, 0, part)
            with sp.Fori(0, ITER - 1) as it:
                step(it, True)
            step(ITER - 1, False)
            for r in range(2):
                sp.wait_ge(stored[r], 16 * ITER * C // 2 + START)

        @block.tensor
        def _(pe):
            def scores(it, n):
                c, kb, start, _ = unit(n)
                slot, ch = n // U, chunk_of(n)
                if first(n):
                    pe.wait_ge(k_loaded[slot][ch % NW > 0], it * 64 + 64 + START)
                    pe.wait_ge(q_loaded[ch % 2], it * (32 * NW) + (ch // 2 + 1) * 32 + START)
                t0, tn = key_block(kb)
                for h, name in enumerate(("w_0_ready", "w_ready")):
                    await_units(pe, name, it, bank_before(n) + 1)
                    for part, k in enumerate((k_high, k_low)):
                        mm = nc.tensor.matmul(z[bank(n)][0:tn, h, start:W], k[slot][:, h, t0:t0 + tn],
                                              q[ch % 2][:, h, start:W], start=(part == 0), stop=(part == 1),
                                              skip_group_check=True)
                    if diagonal(n):
                        mm = nc.tensor.matmul(z[bank(n)][:, h, start:start + P], ident[:, :], never[:, :],
                                              start=False, stop=True, skip_group_check=True)
                done("z_ready", mm)

            def subtract_sums(it, n):
                _, kb, start, prev = unit(n)
                tn = rows(n)

                def add(h, lhs, tile, kk, lo):
                    return nc.tensor.matmul(z[bank(n)][0:tn, h, lo:W], lhs, tile[bank(n)][0:kk, h, lo:W],
                                            start=False, stop=True, skip_group_check=True)

                await_units(pe, "sp_ready", it, n + 1)
                if tn < P:
                    await_units(pe, "high_ready", it, n + 1)
                    await_units(pe, "low_ready", it, n + 1)
                if carried(n):
                    await_units(pe, "newer_ready", it, having(carried, n + 1), CARRIED)
                    for h in range(2):
                        add(h, plain[:, 1, 0:tn], newer, P, prev)
                for h, name in enumerate(("summed_0", "summed")):
                    if h == 0 and tn == P:
                        await_units(pe, "high_ready", it, n + 1)
                    add(h, minus[0:tn, :tn], sp_hi, tn, start)
                    if h == 0 and tn == P:
                        await_units(pe, "low_ready", it, n + 1)
                    done(name, add(h, minus[0:tn, :tn], sp_lo, tn, start))

            def apply(it, n):
                _, kb, start, _ = unit(n)
                slot, ch, tn = n // U, chunk_of(n), rows(n)
                if first(n):
                    loads = 16 if ch % NW else 32
                    pe.wait_ge(v_loaded[slot][ch % NW > 0], it * loads + loads + START)
                    await_units(pe, "out_ready", it, ch - 1, C)
                await_units(pe, "w_ready", it, n + 1)
                for h in range(2):
                    mm = nc.tensor.matmul(o[ch % 2][h * HEAD:(h + 1) * HEAD, start:W],
                                          v[slot][0:tn, kb, h * HEAD:(h + 1) * HEAD], w[bank(n)][0:tn, h, start:W],
                                          start=first(n), stop=last(n), skip_group_check=True)
                done("applied", mm)

            pe.wait_ge(minus_ready, START + 1)
            pe.wait_ge(made, START + 3)
            with pe.Fori(0, ITER) as it:
                for n in range(-RING, N + 1):
                    if 0 <= n < N:
                        subtract_sums(it, n)
                    if n >= 1:
                        apply(it, n - 1)
                    if n + RING < N:
                        scores(it, n + RING)

        @block.scalar
        def _(act):
            nc.scalar.preload_act_table_set(EXP_AND_LN)
            act.wait_ge(made, START + 3)
            nc.scalar.activation(minus[:, :], plain[:, 0, :], ACT.Copy).then_inc(minus_ready, 1)

            def exp_scores(it, n):
                await_units(act, "z_ready", it, n + 1)
                await_units(act, "sp_ready", it, bank_before(n) + 1)
                done("exp_ready", nc.scalar.activation(columns(soft[bank(n)], n), columns(z[bank(n)], n), ACT.Exp))

            def ln(it, n):
                await_units(act, "capped", it, n + 1)
                tile = columns(soft[bank(n)], n)
                done("ln_ready", nc.scalar.activation(tile, tile, ACT.Ln, bias=1.0))

            def weights(it, n):
                start, tn = unit(n)[2], rows(n)
                await_units(act, "applied", it, bank_before(n) + 1)
                for h, (sums, ready) in enumerate((("summed_0", "w_0_ready"), ("summed", "w_ready"))):
                    await_units(act, sums, it, n + 1)
                    done(ready, nc.scalar.activation(w[bank(n)][0:tn, h, start:W], z[bank(n)][0:tn, h, start:W],
                                                     ACT.Exp))

            with act.Fori(0, ITER) as it:
                for n in range(-2, N):
                    if 0 <= n + 1 < N:
                        ln(it, n + 1)
                    if n + 2 < N:
                        exp_scores(it, n + 2)
                    if n >= 0:
                        weights(it, n)

        @block.vector
        def _(dve):
            def cap(it, n):
                await_units(dve, "exp_ready", it, n + 1)
                tile = columns(soft[bank(n)], n)
                done("capped", nc.vector.tensor_scalar(tile, tile, LN_TOP, None, ALU.min))

            def softplus(it, n):
                await_units(dve, "ln_ready", it, n + 1)
                await_units(dve, "newer_ready", it, having(carried, bank_before(n) + 2), CARRIED)
                tile = sp_[bank(n)]
                mx = nc.vector.tensor_tensor(columns(tile, n), columns(soft[bank(n)], n), columns(z[bank(n)], n), ALU.max)
                done("sp_ready", mx)

            def split(it, n):
                await_units(dve, "sp_ready", it, n + 1)
                await_units(dve, "summed", it, bank_before(n) + 1)
                done("high_ready", nc.vector.tensor_copy(columns(sp_hi[bank(n)], n), columns(sp_[bank(n)], n)))
                await_units(dve, "high_ready", it, n + 1)
                done("low_ready", nc.vector.tensor_tensor(columns(sp_lo[bank(n)], n), columns(sp_[bank(n)], n),
                                                          columns(sp_hi[bank(n)], n).bitcast(F32), ALU.subtract))

            def gated(it, n):
                ch = chunk_of(n)
                await_units(dve, "applied", it, n + 1)
                dve.wait_ge(gate_loaded[ch % 2], it * (16 * NW) + (ch // 2 + 1) * 16 + START)
                dve.wait_ge(stored[ch % 2], it * (16 * NW) + ch // 2 * 16 + START)
                done("out_ready", nc.vector.tensor_tensor(out[ch % 2][:, :], gate[ch % 2][:, :], o[ch % 2][:, :], ALU.mult))

            with dve.Fori(0, ITER) as it:
                for n in range(-2, N + 2):
                    if n + 2 < N:
                        cap(it, n + 2)
                    if 0 <= n + 1 < N:
                        softplus(it, n + 1)
                        split(it, n + 1)
                    if n >= 2 and last(n - 2):
                        gated(it, n - 2)

        @block.gpsimd
        def _(pool):
            nc.gpsimd.memset(plain[:, :, :], -1.0).then_inc(filled, 1)
            nc.gpsimd.memset(ident[:, :], 0.0).then_inc(filled, 1)
            nc.gpsimd.memset(never[:, :], 0.0).then_inc(filled, 1)
            nc.gpsimd.memset(zero[:, :], 0.0).then_inc(filled, 1)
            pool.wait_ge(filled, START + 4)
            nc.gpsimd.affine_select(out=plain[:, 0, :], in_=plain[:, 0, :], compare_op=ALU.is_ge, fill=0.0, base=0,
                                    pattern=[[-1, P]], channel_multiplier=1).then_inc(made, 1)
            nc.gpsimd.affine_select(out=ident[:, :], in_=ident[:, :], compare_op=ALU.not_equal, fill=1.0, base=0,
                                    pattern=[[-1, P]], channel_multiplier=1).then_inc(made, 1)
            nc.gpsimd.affine_select(out=never[:, :], in_=never[:, :], compare_op=ALU.is_gt, fill=NEVER, base=0,
                                    pattern=[[1, P]], channel_multiplier=-1).then_inc(made, 1)

            def sum_newer(it, n):
                new, old, add = newer[bank(n)], newer[bank(n - 1)], sp_[bank(n - 1)]
                prev, before = unit(n)[3], unit(n - 1)[3]
                await_units(pool, "sp_ready", it, n)
                await_units(pool, "summed", it, bank_before(n) + 1)
                await_units(pool, "newer_ready", it, having(carried, n), CARRIED)
                def taken(lo, hi):
                    return nc.gpsimd.tensor_tensor(new[:, :, lo:hi], add[:, :, lo:hi],
                                                   zero[:, :].unsqueeze(2).to_broadcast([P, 2, hi - lo]), ALU.add)

                if before is None:
                    mm = taken(prev, W)
                else:
                    if before > prev:
                        taken(prev, before)
                    mm = nc.gpsimd.tensor_tensor(new[:, :, before:W], old[:, :, before:W], add[:, :, before:W], ALU.add)
                done("newer_ready", mm)

            with pool.Fori(0, ITER) as it:
                for n in range(-1, N):
                    if n + 1 < N and carried(n + 1):
                        sum_newer(it, n + 1)


def output_stage(nc, scratch, x, w_out, group_w, final_w, out):
    with ExitStack() as ctx:
        m = Memory(nc, ctx)
        NH = D // W
        w_hi = m.sbuf("o_w_hi", [P, MB, D], F32R)
        w_lo = m.sbuf("o_w_lo", [P, MB, D], F32R)
        g = [m.sbuf(f"o_g{s}", [P, MB, P]) for s in range(2)]
        g_hi = [m.sbuf(f"o_g_hi{s}", [P, MB, P], F32R) for s in range(2)]
        g_lo = [m.sbuf(f"o_g_lo{s}", [P, MB, P], F32R) for s in range(2)]
        squares = m.sbuf("o_squares", [P, D])
        sq_sum = [m.sbuf(f"o_sq_sum{s}", [P, 2, P]) for s in range(2)]
        h = [m.sbuf(f"o_h{s}", [P, D]) for s in range(2)]
        y = [m.sbuf(f"o_y{s}", [P, D]) for s in range(2)]
        gw = m.sbuf("o_gw", [P, MB])
        fw = m.sbuf("o_fw", [P, D])
        ones, power = m.sbuf("o_ones", [P, 1]), m.sbuf("o_power", [P, 2])
        var = [m.sbuf(f"o_var{s}", [P, 2]) for s in range(2)]
        rstd = [m.sbuf(f"o_rstd{s}", [P, 2]) for s in range(2)]
        f_ssq = [m.sbuf(f"o_f_ssq{s}", [P, 1]) for s in range(2)]
        f_var = [m.sbuf(f"o_f_var{s}", [P, 1]) for s in range(2)]
        f_rstd = [m.sbuf(f"o_f_rstd{s}", [P, 1]) for s in range(2)]
        pss = m.psum("o_pss", [P, 2])
        acc = [[m.psum(f"o_acc{n}{q}", [P, W]) for q in range(2)] for n in range(NH)]

        made, small_loaded = m.sem("o_made"), m.sem("o_small_loaded")
        w_loaded, w_high, w_low = m.sems("o_w_loaded", 2), m.sem("o_w_high"), m.sem("o_w_low")
        g_loaded, h_loaded = m.sems("g_loaded", 2), m.sems("h_loaded", 2)
        squared = [m.sems(f"squared{s}", 2) for s in range(2)]
        reduced = [m.sems(f"reduced{s}", 2) for s in range(2)]
        weighed, g_high, g_low = m.sems("weighed", 2), m.sems("g_high", 2), m.sems("g_low", 2)
        ssq_ready, var_ready, rstd_ready = m.sems("o_ssq_ready", 2), m.sems("o_var_ready", 2), m.sems("o_rstd_ready", 2)
        acc_ready = [[m.sems(f"o_acc_ready{s}{n}", 2) for n in range(NH)] for s in range(2)]
        half_added = [m.sems(f"half_added{s}", NH) for s in range(2)]
        added = [m.sems(f"added{s}", NH) for s in range(2)]
        f_ssq_ready, f_var_ready, f_rstd_ready = (m.sems(n, 2) for n in ("f_ssq_ready", "f_var_ready", "f_rstd_ready"))
        y_ready, stored = m.sems("y_ready", 2), m.sems("o_stored", 2)
        m.start()
        block = ctx.enter_context(nc.Block())
        LOOPS = NT // 2

        def pipeline(eng, front, back):
            front(0, 0)

            def body(i, more):
                front(1, i)
                back(0, i)
                if more:
                    front(0, i + 1)
                back(1, i)

            with eng.Fori(0, LOOPS - 1) as i:
                body(i, True)
            body(LOOPS - 1, False)

        @block.sync
        def _(sp):
            sp.dma_start(gw[:, :], group_w).then_inc(small_loaded, 16)
            sp.dma_start(fw[:, :], final_w.to_broadcast([P, D])).then_inc(small_loaded, 16)

            def load(s, i):
                col = i * (2 * P) + s * P
                sp.dma_start(g[s][:, :, :], scratch["mixed"][:, :, bass.ds(col, P)]
                             .rearrange("b p t -> p b t")).then_inc(g_loaded[s], 16)
                sp.dma_start(h[s][:, :], x[0, bass.ds(col, P), :]).then_inc(h_loaded[s], 16)

            for k in range(MB):
                if k >= 2:
                    sp.wait_ge(w_high, k - 1 + START)
                    sp.wait_ge(w_low, k - 1 + START)
                sp.dma_start(y[k % 2][:, :], w_out[:, k, :]).then_inc(w_loaded[k % 2], 16)
                if k < 2:
                    load(k, 0)

            def step(i, more):
                for s in range(2):
                    sp.wait_ge(y_ready[s], i + 1 + START)
                    sp.dma_start(out[0, bass.ds(i * (2 * P) + s * P, P), :], y[s][:, :]).then_inc(stored[s], 16)
                    if more:
                        load(s, i + 1)

            with sp.Fori(0, LOOPS - 1) as i:
                step(i, True)
            step(LOOPS - 1, False)
            for s in range(2):
                sp.wait_ge(stored[s], 16 * LOOPS + START)

        @block.gpsimd
        def _(pool):
            nc.gpsimd.memset(ones[:, :], 1.0).then_inc(made, 1)
            nc.gpsimd.memset(power[:, :], -0.5).then_inc(made, 1)
            pool.wait_ge(made, START + 2)

            def back(s, i):
                pool.wait_ge(var_ready[s], i + 1 + START)
                nc.gpsimd.tensor_tensor(rstd[s][:, :], var[s][:, :], power[:, :], ALU.pow).then_inc(rstd_ready[s], 1)
                pool.wait_ge(f_var_ready[s], i + 1 + START)
                nc.gpsimd.tensor_tensor(f_rstd[s][:, :], f_var[s][:, :], power[:, 0:1], ALU.pow).then_inc(f_rstd_ready[s], 1)

            pipeline(pool, lambda s, i: None, back)

        @block.tensor
        def _(pe):
            pe.wait_ge(made, START + 2)
            pe.wait_ge(w_high, MB + START)
            pe.wait_ge(w_low, MB + START)

            def back(s, i):
                pe.wait_ge(var_ready[1 - s], i + s + START)
                for q in range(2):
                    pe.wait_ge(reduced[s][q], i + 1 + START)
                    last = nc.tensor.matmul(pss[:, q:q + 1], sq_sum[s][:, q, :], ones[:, :], start=True, stop=True)
                last.then_inc(ssq_ready[s], 1)
                pe.wait_ge(g_high[s], i + 1 + START)
                pe.wait_ge(g_low[s], i + 1 + START)
                for n in range(NH):
                    pe.wait_ge(added[1 - s][n], i + s + START)
                    for q in range(2):
                        for k in range(q * KB, (q + 1) * KB):
                            for lhs, rhs in ((g_hi, w_hi), (g_hi, w_lo), (g_lo, w_hi)):
                                last = nc.tensor.matmul(acc[n][q][:, :], lhs[s][:, k, :], rhs[:, k, n * W:(n + 1) * W],
                                                        start=(k == q * KB and lhs is g_hi and rhs is w_hi),
                                                        stop=(k == (q + 1) * KB - 1 and lhs is g_lo))
                        last.then_inc(acc_ready[s][n][q], 1)

            pipeline(pe, lambda s, i: None, back)

        @block.scalar
        def _(act):
            for k in range(MB):
                act.wait_ge(w_loaded[k % 2], 16 * (k // 2 + 1) + START)
                nc.scalar.activation(w_hi[:, k, :], y[k % 2][:, :], ACT.Copy).then_inc(w_high, 1)

            def front(s, i):
                act.wait_ge(g_loaded[s], i * 16 + 16 + START)
                for q in range(2):
                    if q:
                        act.wait_ge(reduced[s][0], i + 1 + START)
                    else:
                        act.wait_ge(reduced[1 - s][1], i + s + START)
                    nc.scalar.activation(squares[:, :], g[s][:, q * KB:(q + 1) * KB, :].rearrange("p b t -> p (b t)"),
                                         ACT.Square).then_inc(squared[s][q], 1)
                act.wait_ge(weighed[s], i + 1 + START)
                act.wait_ge(acc_ready[s][NH - 1][1], i + START)
                nc.scalar.activation(g_hi[s][:, :, :], g[s][:, :, :], ACT.Copy).then_inc(g_high[s], 1)

            def back(s, i):
                act.wait_ge(added[s][NH - 1], i + 1 + START)
                nc.scalar.activation(h[s][:, :], y[s][:, :], ACT.Square,
                                     accum_out=f_ssq[s][:, :]).then_inc(f_ssq_ready[s], 1)

            pipeline(act, front, back)

        @block.vector
        def _(dve):
            for k in range(MB):
                dve.wait_ge(w_high, k + 1 + START)
                nc.vector.tensor_tensor(w_lo[:, k, :], y[k % 2][:, :], w_hi[:, k, :].bitcast(F32),
                                        ALU.subtract).then_inc(w_low, 1)
            dve.wait_ge(small_loaded, START + 32)

            def front(s, i):
                for q in range(2):
                    dve.wait_ge(squared[s][q], i + 1 + START)
                    if q == 0:
                        dve.wait_ge(ssq_ready[s], i + START)
                    nc.vector.tensor_reduce(sq_sum[s][:, q, :], squares[:, :].rearrange("p (b t) -> p t b", b=KB),
                                            mybir.AxisListType.X, ALU.add).then_inc(reduced[s][q], 1)
                nc.vector.tensor_tensor(g[s][:, :, :], g[s][:, :, :], spread(gw[:, :], P), ALU.mult).then_inc(weighed[s], 1)
                dve.wait_ge(g_high[s], i + 1 + START)
                nc.vector.tensor_tensor(g_lo[s][:, :, :], g[s][:, :, :], g_hi[s][:, :, :].bitcast(F32),
                                        ALU.subtract).then_inc(g_low[s], 1)

            def back(s, i):
                dve.wait_ge(ssq_ready[s], i + 1 + START)
                nc.vector.tensor_scalar(var[s][:, :], pss[:, :], 1.0 / D, EPS, ALU.mult, ALU.add).then_inc(var_ready[s], 1)
                dve.wait_ge(rstd_ready[s], i + 1 + START)
                dve.wait_ge(h_loaded[s], i * 16 + 16 + START)
                dve.wait_ge(stored[s], i * 16 + START)
                for n in range(NH):
                    cols = slice(n * W, (n + 1) * W)
                    dve.wait_ge(acc_ready[s][n][0], i + 1 + START)
                    nc.vector.scalar_tensor_tensor(out=y[s][:, cols], in0=acc[n][0][:, :], scalar=rstd[s][:, 0:1],
                                                   in1=h[s][:, cols], op0=ALU.mult, op1=ALU.add).then_inc(half_added[s][n], 1)
                    dve.wait_ge(half_added[s][n], i + 1 + START)
                    dve.wait_ge(acc_ready[s][n][1], i + 1 + START)
                    nc.vector.scalar_tensor_tensor(out=y[s][:, cols], in0=acc[n][1][:, :], scalar=rstd[s][:, 1:2],
                                                   in1=y[s][:, cols], op0=ALU.mult, op1=ALU.add).then_inc(added[s][n], 1)
                dve.wait_ge(f_ssq_ready[s], i + 1 + START)
                nc.vector.tensor_scalar(f_var[s][:, :], f_ssq[s][:, :], 1.0 / D, EPS, ALU.mult,
                                        ALU.add).then_inc(f_var_ready[s], 1)
                dve.wait_ge(f_rstd_ready[s], i + 1 + START)
                nc.vector.scalar_tensor_tensor(out=y[s][:, :], in0=y[s][:, :], scalar=f_rstd[s][:, :], in1=fw[:, :],
                                               op0=ALU.mult, op1=ALU.mult).then_inc(y_ready[s], 1)

            pipeline(dve, front, back)


def hybrid_block(nc, x, meta, norm_w, w_blocks, w_dt, conv_wb, dt_cols, d_cols, group_w, w_out, final_w, out):
    shapes = {"k_hi": [PAIRS, P, T], "k_lo": [PAIRS, P, T], "q_hi": [PAIRS, P, SEQ], "q_lo": [PAIRS, P, SEQ],
              "xbc": [XB, P, T], "gate": [MB, P, SEQ], "v": [T, D], "mixed": [MB, P, SEQ]}
    scratch = {name: nc.dram_tensor(f"scratch_{name}", shape, F32, kind="Internal").ap() for name, shape in shapes.items()}
    with ExitStack() as ctx:
        dt_tok = ctx.enter_context(nc.sbuf_tensor("dt_tok", [P, NT + 1, 2, HEADS], F32))
        with ExitStack() as of_u:
            ut_hi = of_u.enter_context(nc.sbuf_tensor("ut_hi", [P, KB, T], F32R))
            ut_lo = of_u.enter_context(nc.sbuf_tensor("ut_lo", [P, KB, T], F32R))
            norm_stage(nc, x, meta, norm_w, ut_hi, ut_lo)
            feature_stage(nc, w_blocks, conv_wb, ut_hi, ut_lo, scratch)
            token_stage(nc, w_blocks, w_dt, dt_cols, ut_hi, ut_lo, dt_tok, scratch)
        with ExitStack() as of_state:
            state = of_state.enter_context(nc.sbuf_tensor("state", [P, GROUPS, W], F32))
            scan_start(nc, scratch, dt_tok, state)
            scan_stage(nc, scratch, d_cols, dt_tok, state)
    attention_stage(nc, scratch)
    output_stage(nc, scratch, x, w_out, group_w, final_w, out)


def kernel(x, meta_tokens, norm_w, w_in, conv_w, conv_b, dt_bias, a_log, d_skip, sb_norm_w, ssd_norm_w, w_out,
           final_norm_w):
    import numpy as np
    import concourse.bacc as bacc
    from concourse.bass_utils import run_bass_kernel_spmd

    def rows(a, b):
        return np.asarray(a).reshape(b, P).T

    w = np.asarray(w_in)[0]
    edges = np.cumsum([0, D, D, D, D, D, XBC, HEADS])
    q, k, v, sb_gate, z, xbc, dt = (w[:, a:b] for a, b in zip(edges[:-1], edges[1:]))

    def blocks(a):
        return a.reshape(KB, P, -1, P).transpose(2, 1, 0, 3)

    arrays = {
        "x": np.asarray(x),
        "meta": np.asarray(meta_tokens),
        "norm_w": rows(norm_w, KB),
        "w_blocks": np.concatenate([blocks(a) for a in (k, xbc, q, sb_gate, z, v)]),
        "w_dt": dt.reshape(KB, P, HEADS).transpose(1, 0, 2),
        "conv_wb": np.concatenate([np.asarray(conv_w)[0], np.asarray(conv_b)]).T.reshape(XB, P, CONV + 1),
        "dt_cols": np.stack([np.asarray(dt_bias)[0], np.asarray(a_log)[0]], axis=1),
        "d_cols": rows(np.repeat(np.asarray(d_skip)[0], HEAD), KB),
        "group_w": np.concatenate([rows(sb_norm_w, KB), rows(ssd_norm_w, KB)], axis=1),
        "w_out": np.asarray(w_out)[0].reshape(MB, P, D).transpose(1, 0, 2),
        "final_w": np.asarray(final_norm_w).reshape(1, D),
    }
    nc = bacc.Bacc("TRN2", target_bir_lowering=False, num_devices=1)
    args, feed = [], {}
    for name, array in arrays.items():
        feed[f"in_{name}"] = np.ascontiguousarray(array)
        args.append(nc.dram_tensor(f"in_{name}", array.shape, F32, kind="ExternalInput").ap())
    out = nc.dram_tensor("out_y", [1, SEQ, D], F32, kind="ExternalOutput").ap()
    hybrid_block(nc, *args, out)
    return run_bass_kernel_spmd(nc, [feed], core_ids=[0]).results[0]["out_y"]
```

```python
from contextlib import ExitStack

import concourse.bass as bass
from concourse import mybir

ALU = mybir.AluOpType
ACT = mybir.ActivationFunctionType
F32 = mybir.dt.float32
F32R = mybir.dt.float32r
BF16 = mybir.dt.bfloat16

P = 128
D = 1024
KB = D // P
SEQ = 2048
META = 16
T = META + SEQ
NT = SEQ // P
W = 512
NW = SEQ // W
HEAD = 64
HEADS = 16
PAIRS = HEADS // 2
STATE = 128
GROUPS = 2
HPG = HEADS // GROUPS
CONV = 4
XBC = D + 2 * GROUPS * STATE
XB = XBC // P
EPS = 1e-5
START = 4
K_BLOCK, X_BLOCK = 0, PAIRS
Q_BLOCK = X_BLOCK + XB
G_BLOCK = Q_BLOCK + PAIRS
V_BLOCK = G_BLOCK + 2 * KB
MB = 2 * KB
CHUNKS = [(0, META)] + [(META + W * c, W) for c in range(NW)]
EXP_AND_LN = "natural_log_exp_and_others"
Q_SCALE = HEAD ** -0.5
NEVER = -(2.0 ** 100)
LN_TOP = float(2 ** 60)


class Memory:

    def __init__(self, nc, ctx):
        self.nc, self.ctx, self.semaphores = nc, ctx, []
        ctx.callback(self.clear)

    def start(self):
        nc = self.nc
        engines = (nc.sync, nc.gpsimd, nc.scalar, nc.vector, nc.tensor)
        for n, sem in enumerate(self.semaphores):
            engines[n % len(engines)].sem_inc(sem, START)
        nc.all_engine_barrier()

    def clear(self):
        self.nc.clear_and_free_semaphores(self.semaphores)
        self.nc.all_engine_barrier()

    def sbuf(self, name, shape, dt=F32):
        return self.ctx.enter_context(self.nc.sbuf_tensor(name, shape, dt))

    def psum(self, name, shape, dt=F32):
        return self.ctx.enter_context(self.nc.psum_tensor(name, shape, dt))

    def sem(self, name):
        self.semaphores.append(self.nc.alloc_semaphore(name))
        return self.semaphores[-1]

    def sems(self, name, n):
        return [self.sem(f"{name}_{i}") for i in range(n)]


def spread(column_block, n):
    return column_block.unsqueeze(2).to_broadcast([column_block.shape[0], column_block.shape[1], n])


def norm_stage(nc, x, meta, norm_w, ut_hi, ut_lo):
    with ExitStack() as ctx:
        m = Memory(nc, ctx)
        SLOTS = 4
        LOOPS = NT // SLOTS
        ident = m.sbuf("n_ident", [P, P])
        nw = m.sbuf("n_nw", [P, KB])
        power = m.sbuf("n_power", [P, 1])
        xin = [m.sbuf(f"n_xin{s}", [P, D]) for s in range(SLOTS)]
        xn = [m.sbuf(f"n_xn{s}", [P, D]) for s in range(SLOTS)]
        un = [m.sbuf(f"n_un{s}", [P, KB, P]) for s in range(SLOTS)]
        ssq = [m.sbuf(f"n_ssq{s}", [P, 1]) for s in range(SLOTS)]
        var = [m.sbuf(f"n_var{s}", [P, 1]) for s in range(SLOTS)]
        rstd = [m.sbuf(f"n_rstd{s}", [P, 1]) for s in range(SLOTS)]
        pt = [m.psum(f"n_pt{s}", [P, KB, P]) for s in range(SLOTS)]
        nw_loaded, ident_zero, ident_ready = m.sem("nw_loaded"), m.sem("ident_zero"), m.sem("ident_ready")
        x_loaded = m.sems("x_loaded", SLOTS)
        ssq_ready = m.sems("ssq_ready", SLOTS)
        var_ready = m.sems("var_ready", SLOTS)
        rstd_ready = m.sems("rstd_ready", SLOTS)
        xn_ready = m.sems("xn_ready", SLOTS)
        turned = m.sems("turned", SLOTS)
        un_ready = m.sems("un_ready", SLOTS)
        hi_ready = m.sems("hi_ready", SLOTS)
        lo_ready = m.sems("lo_ready", SLOTS)
        m.start()
        block = ctx.enter_context(nc.Block())

        def is_meta(i):
            return isinstance(i, int) and i == LOOPS

        def rows(i):
            return META if is_meta(i) else P

        def columns(tile, s, i):
            if is_meta(i):
                return tile[:, :, 0:META]
            return tile[:, :, bass.ds(i * (SLOTS * P) + (META + s * P), P)]

        def pipeline(eng, *stages):
            def step(i, j):
                for ahead, do in stages:
                    shift, s = (j + ahead) // SLOTS, (j + ahead) % SLOTS
                    at = i + shift if shift else i
                    if not isinstance(at, int) or 0 <= at < LOOPS or (at, s) == (LOOPS, 0):
                        do(s, at)

            for j in range(-3, SLOTS):
                step(0, j)
            with eng.Fori(1, LOOPS - 1) as i:
                for j in range(SLOTS):
                    step(i, j)
            for j in range(SLOTS + 2):
                step(LOOPS - 1, j)

        @block.sync
        def _(sp):
            def load(s, i):
                src = meta[:, :] if is_meta(i) else x[0, bass.ds(i * (SLOTS * P) + s * P, P), :]
                sp.wait_ge(xn_ready[s], i + START)
                sp.dma_start(xin[s][0:rows(i), :], src).then_inc(x_loaded[s], 16)

            for s in range(SLOTS):
                load(s, 0)
            sp.dma_start(nw[:, :], norm_w).then_inc(nw_loaded, 16)
            with sp.Fori(1, LOOPS) as i:
                for s in range(SLOTS):
                    load(s, i)
            load(0, LOOPS)

        @block.gpsimd
        def _(pool):
            nc.gpsimd.memset(ident[:, :], 0.0).then_inc(ident_zero, 1)
            nc.gpsimd.memset(power[:, :], -0.5).then_inc(ident_zero, 1)
            pool.wait_ge(ident_zero, START + 2)
            nc.gpsimd.affine_select(out=ident[:, :], in_=ident[:, :], compare_op=ALU.not_equal, fill=1.0,
                                    base=0, pattern=[[-1, P]], channel_multiplier=1).then_inc(ident_ready, 1)

            def root(s, i):
                n = rows(i)
                pool.wait_ge(var_ready[s], i + 1 + START)
                nc.gpsimd.tensor_tensor(rstd[s][0:n, :], var[s][0:n, :], power[0:n, :], ALU.pow).then_inc(rstd_ready[s], 1)

            pipeline(pool, (0, root))

        @block.scalar
        def _(act):
            def square(s, i):
                n = rows(i)
                act.wait_ge(x_loaded[s], i * 16 + 16 + START)
                act.wait_ge(turned[s], i + START)
                nc.scalar.activation(xn[s][0:n, :], xin[s][0:n, :], ACT.Square,
                                     accum_out=ssq[s][0:n, :]).then_inc(ssq_ready[s], 1)

            def high(s, i):
                act.wait_ge(un_ready[s], i + 1 + START)
                nc.scalar.copy(columns(ut_hi, s, i), un[s][:, :, 0:rows(i)]).then_inc(hi_ready[s], 1)

            pipeline(act, (3, square), (0, high))

        @block.vector
        def _(dve):
            def variance(s, i):
                n = rows(i)
                dve.wait_ge(ssq_ready[s], i + 1 + START)
                nc.vector.tensor_scalar(var[s][0:n, :], ssq[s][0:n, :], 1.0 / D, EPS, ALU.mult, ALU.add).then_inc(var_ready[s], 1)

            def normalise(s, i):
                n = rows(i)
                dve.wait_ge(rstd_ready[s], i + 1 + START)
                dve.wait_ge(turned[s], i + START)
                nc.vector.tensor_scalar(xn[s][0:n, :], xin[s][0:n, :], rstd[s][0:n, :], None, ALU.mult).then_inc(xn_ready[s], 1)

            def weigh(s, i):
                n = rows(i)
                dve.wait_ge(turned[s], i + 1 + START)
                dve.wait_ge(lo_ready[s], i + START)
                nc.vector.tensor_tensor(un[s][:, :, 0:n], pt[s][:, :, 0:n], spread(nw[:, :], n),
                                        ALU.mult).then_inc(un_ready[s], 1)

            def low(s, i):
                dve.wait_ge(hi_ready[s], i + 1 + START)
                nc.vector.tensor_tensor(columns(ut_lo, s, i), un[s][:, :, 0:rows(i)], columns(ut_hi, s, i).bitcast(F32),
                                        ALU.subtract).then_inc(lo_ready[s], 1)

            dve.wait_ge(nw_loaded, START + 16)
            pipeline(dve, (3, variance), (0, weigh), (2, normalise), (-1, low))

        @block.tensor
        def _(pe):
            pe.wait_ge(ident_ready, START + 1)

            def turn(s, i):
                n = rows(i)
                pe.wait_ge(xn_ready[s], i + 1 + START)
                pe.wait_ge(un_ready[s], i + START)
                for b in range(KB):
                    last = nc.tensor.transpose(pt[s][:, b, 0:n], xn[s][0:n, b * P:(b + 1) * P], ident[0:n, 0:n])
                last.then_inc(turned[s], 1)

            pipeline(pe, (0, turn))


def feature_stage(nc, w_blocks, conv_wb, ut_hi, ut_lo, scratch):
    with ExitStack() as ctx:
        m = Memory(nc, ctx)
        LEAD = CONV
        NC = len(CHUNKS)
        LAST = NC - 1
        stage = [m.sbuf(f"f_stage{s}", [P, KB, P]) for s in range(2)]
        w_hi = [m.sbuf(f"f_w_hi{s}", [P, KB, P], F32R) for s in range(2)]
        w_lo = [m.sbuf(f"f_w_lo{s}", [P, KB, P], F32R) for s in range(2)]
        row_a = [m.sbuf(f"f_row_a{s}", [P, LEAD + T]) for s in range(2)]
        row_b = [m.sbuf(f"f_row_b{s}", [P, LEAD + T]) for s in range(2)]
        zero = m.sbuf("f_zero", [P, 1])
        taps = [m.sbuf(f"f_taps{s}", [P, CONV + 1]) for s in range(2)]
        acc = [m.psum(f"f_acc{c}", [P, W]) for c in range(NC)]
        w_loaded = m.sems("w_loaded", 2)
        w_split = m.sems("w_split", 2)
        acc_ready = [m.sems(f"acc_ready{s}", NC) for s in range(2)]
        acc_high = [m.sems(f"acc_high{s}", NC) for s in range(2)]
        acc_freed = [m.sems(f"acc_freed{s}", NC) for s in range(2)]
        taps_loaded = m.sems("taps_loaded", 2)
        lead_zero, zeroed = m.sem("lead_zero"), m.sem("zeroed")
        conv_step = m.sems("conv_step", 2)
        silu_done = m.sems("silu_done", 2)
        stored = m.sems("f_stored", 2)
        m.start()
        block = ctx.enter_context(nc.Block())

        KINDS = [("k", K_BLOCK, PAIRS, 0, ("k_hi", "k_lo")), ("conv", X_BLOCK, XB, 0, ("xbc",)),
                 ("q", Q_BLOCK, PAIRS, 1, ("q_hi", "q_lo")), ("gate", G_BLOCK, MB, 1, ("gate",))]
        TOTAL = V_BLOCK

        def stores_before(kind):
            done = 0
            for name, _, n, _, outs in KINDS:
                if name == kind:
                    return done
                done += n // 2 * len(outs)
            return done

        @block.sync
        def _(sp):
            def load(s, number):
                sp.dma_start(stage[s][:, :, :], w_blocks[bass.ds(number, 1), :, :, :]
                             .rearrange("b p k c -> (b p) k c")).then_inc(w_loaded[s], 16)

            load(0, 0)
            load(1, 1)
            for kind, b0, n, c0, outs in KINDS:
                first = CHUNKS[c0][0]

                def step(i, s, more):
                    j = i + b0 // 2
                    if kind == "conv":
                        sp.wait_ge(silu_done[s], i + 1 + START)
                    else:
                        sp.wait_ge(acc_freed[s][LAST], j + 1 + START)
                    for name, row in zip(outs, (row_a[s], row_b[s])):
                        sp.dma_start(scratch[name][bass.ds(i * 2 + s, 1), :, :].rearrange("b p t -> (b p) t"),
                                     row[:, LEAD + first:LEAD + T]).then_inc(stored[s], 16)
                    if more:
                        sp.wait_ge(w_split[s], (j + 1) * 2 + START)
                        load(s, i * 2 + (b0 + s + 2))

                peel = kind == KINDS[-1][0]
                with sp.Fori(0, n // 2 - peel) as i:
                    for s in range(2):
                        step(i, s, True)
                if peel:
                    for s in range(2):
                        step(n // 2 - 1, s, False)
            for s in range(2):
                sp.wait_ge(stored[s], 16 * (stores_before("gate") + MB // 2) + START)

        @block.gpsimd
        def _(pool):
            for s in range(2):
                nc.gpsimd.memset(row_a[s][:, 0:LEAD], 0.0).then_inc(lead_zero, 1)
            nc.gpsimd.memset(zero[:, :], 0.0).then_inc(zeroed, 1)
            pool.wait_ge(zeroed, START + 1)
            with pool.Fori(0, TOTAL // 2) as j:
                for s in range(2):
                    pool.wait_ge(w_loaded[s], j * 16 + 16 + START)
                    pool.wait_ge(acc_ready[s][LAST], j + START)
                    nc.gpsimd.tensor_tensor(w_hi[s][:, :, :], stage[s][:, :, :],
                                            spread(zero[:, :], P).to_broadcast([P, KB, P]), ALU.add).then_inc(w_split[s], 1)
                    pool.wait_ge(w_split[s], j * 2 + 1 + START)
                    nc.gpsimd.tensor_tensor(w_lo[s][:, :, :], stage[s][:, :, :], w_hi[s][:, :, :].bitcast(F32),
                                            ALU.subtract).then_inc(w_split[s], 1)

        @block.tensor
        def _(pe):
            for kind, b0, n, c0, _ in KINDS:
                with pe.Fori(0, n // 2) as i:
                    for s in range(2):
                        j = i + b0 // 2
                        pe.wait_ge(w_split[s], j * 2 + 2 + START)
                        for c in range(c0, NC):
                            t0, tn = CHUNKS[c]
                            pe.wait_ge(acc_freed[1 - s][c], j + s + START)
                            for k in range(KB):
                                for w, u in ((w_hi, ut_hi), (w_hi, ut_lo), (w_lo, ut_hi)):
                                    last = nc.tensor.matmul(acc[c][:, 0:tn], w[s][:, k, :], u[:, k, t0:t0 + tn],
                                                            start=(k == 0 and u is ut_hi and w is w_hi),
                                                            stop=(k == KB - 1 and w is w_lo))
                            last.then_inc(acc_ready[s][c], 1)

        @block.scalar
        def _(act):
            for kind, b0, n, c0, outs in KINDS:
                with act.Fori(0, n // 2) as i:
                    for s in range(2):
                        j = i + b0 // 2
                        if kind == "conv":
                            act.dma_start(taps[s][:, :], conv_wb[bass.ds(i * 2 + s, 1), :, :]
                                          .rearrange("b p k -> (b p) k")).then_inc(taps_loaded[s], 16)
                            act.wait_ge(conv_step[s], (i + 1) * CONV + START)
                            nc.scalar.activation(row_a[s][:, LEAD:LEAD + T], row_b[s][:, LEAD:LEAD + T],
                                                 ACT.Silu).then_inc(silu_done[s], 1)
                            continue
                        act.wait_ge(stored[s], (i * len(outs) + stores_before(kind)) * 16 + START)
                        for c in range(c0, NC):
                            t0, tn = CHUNKS[c]
                            to = row_a[s][:, LEAD + t0:LEAD + t0 + tn]
                            act.wait_ge(acc_ready[s][c], j + 1 + START)
                            if kind == "gate":
                                nc.scalar.activation(to, acc[c][:, 0:tn], ACT.Silu).then_inc(acc_freed[s][c], 1)
                            else:
                                nc.scalar.activation(to.bitcast(F32R), acc[c][:, 0:tn], ACT.Copy,
                                                     scale=Q_SCALE if kind == "q" else 1.0).then_inc(acc_high[s][c], 1)

        @block.vector
        def _(dve):
            highs = 0
            for kind, b0, n, c0, outs in KINDS:
                if kind == "gate":
                    continue
                with dve.Fori(0, n // 2) as i:
                    for s in range(2):
                        j = i + b0 // 2
                        if kind == "conv":
                            dve.wait_ge(stored[s], (i * len(outs) + stores_before(kind)) * 16 + START)
                        for c in range(c0, NC):
                            t0, tn = CHUNKS[c]
                            cols = slice(LEAD + t0, LEAD + t0 + tn)
                            if kind == "conv":
                                dve.wait_ge(acc_ready[s][c], j + 1 + START)
                                nc.vector.tensor_copy(row_a[s][:, cols], acc[c][:, 0:tn]).then_inc(acc_freed[s][c], 1)
                            else:
                                dve.wait_ge(acc_high[s][c], i + (highs + 1) + START)
                                nc.vector.scalar_tensor_tensor(
                                    out=row_b[s][:, cols].bitcast(F32R), in0=acc[c][:, 0:tn],
                                    scalar=Q_SCALE if kind == "q" else 1.0, in1=row_a[s][:, cols],
                                    op0=ALU.mult, op1=ALU.subtract).then_inc(acc_freed[s][c], 1)
                        if kind == "conv":
                            dve.wait_ge(acc_freed[s][LAST], j + 1 + START)
                            dve.wait_ge(lead_zero, START + 2)
                            dve.wait_ge(taps_loaded[s], i * 16 + 16 + START)
                            out = row_b[s][:, LEAD:LEAD + T]
                            for tap in range(CONV):
                                shifted = row_a[s][:, 1 + tap:1 + tap + T]
                                if tap == 0:
                                    done = nc.vector.tensor_scalar(out, shifted, taps[s][:, 0:1],
                                                                   taps[s][:, CONV:CONV + 1], ALU.mult, ALU.add)
                                else:
                                    dve.wait_ge(conv_step[s], i * CONV + tap + START)
                                    done = nc.vector.scalar_tensor_tensor(
                                        out=out, in0=shifted, scalar=taps[s][:, tap:tap + 1], in1=out,
                                        op0=ALU.mult, op1=ALU.add)
                                done.then_inc(conv_step[s], 1)
                if kind == "k":
                    highs = n // 2


def token_stage(nc, w_blocks, w_dt, dt_cols, ut_hi, ut_lo, dt_tok, scratch):
    with ExitStack() as ctx:
        m = Memory(nc, ctx)
        RING = 4
        CB = W // P
        stage = m.sbuf("t_stage", [P, CB, KB, P])
        w_hi = m.sbuf("t_w_hi", [P, CB, KB, P], F32R)
        w_lo = m.sbuf("t_w_lo", [P, CB, KB, P], F32R)
        out = [m.sbuf(f"t_out{r}", [P, W]) for r in range(RING + 1)]
        wd = m.sbuf("t_wd", [P, KB, HEADS])
        wd_hi = m.sbuf("t_wd_hi", [P, KB, HEADS], F32R)
        wd_lo = m.sbuf("t_wd_lo", [P, KB, HEADS], F32R)
        dtc = m.sbuf("t_dtc", [HEADS, 2])
        rate = m.sbuf("t_rate", [HEADS, 2])
        ident = m.sbuf("t_ident", [HEADS, HEADS])
        dx, da = m.sbuf("t_dx", [HEADS, W]), m.sbuf("t_da", [HEADS, W])
        de, dl = m.sbuf("t_de", [HEADS, W]), m.sbuf("t_dl", [HEADS, W])
        dt_row, dta_row = m.sbuf("t_dt_row", [HEADS, W]), m.sbuf("t_dta_row", [HEADS, W])
        dacc = [m.psum(f"t_dacc{r}", [P, W]) for r in range(2)]
        dtp = m.psum("t_dtp", [P, CB, 2, HEADS])
        acc = [m.psum(f"t_acc{r}", [P, W]) for r in range(RING + 1)]
        small_loaded, w_loaded = m.sem("t_small_loaded"), m.sem("t_w_loaded")
        ident_zero, ident_ready = m.sem("t_ident_zero"), m.sem("t_ident_ready")
        wd_split, rate_step = m.sem("wd_split"), m.sem("rate_step")
        w_high, w_low = m.sem("t_w_high"), m.sem("t_w_low")
        w_used = m.sem("t_w_used")
        acc_ready = m.sems("t_acc_ready", RING + 1)
        acc_freed = m.sems("t_acc_freed", RING + 1)
        stored = m.sems("t_stored", RING + 1)
        dacc_ready, dx_ready, da_ready = m.sem("dacc_ready"), m.sem("dx_ready"), m.sem("da_ready")
        de_ready, dl_ready, dt_ready, dta_ready = m.sem("de_ready"), m.sem("dl_ready"), m.sem("dt_ready"), m.sem("dta_ready")
        dt_turned, dt_kept = m.sem("dt_turned"), m.sem("dt_kept")
        m.start()
        block = ctx.enter_context(nc.Block())

        PER = NT // RING
        KINDS = [("v", V_BLOCK, True)]
        NCH = D // W

        @block.sync
        def _(sp):
            def load(block):
                sp.dma_start(stage[:, :, :, :], w_blocks[block:block + CB, :, :, :]
                             .rearrange("b p k c -> p b k c")).then_inc(w_loaded, 16)

            sp.dma_start(wd[:, :, :], w_dt).then_inc(small_loaded, 16)
            sp.dma_start(dtc[:, :], dt_cols).then_inc(small_loaded, 16)
            for n, (kind, b0, with_meta) in enumerate(KINDS):
                for i in range(NCH):
                    done = i + n * NCH
                    if done == 0:
                        load(b0)
                    if with_meta:
                        sp.wait_ge(acc_freed[RING], i + 1 + START)
                        sp.dma_start(scratch["v"][0:META, bass.ds(i * W, W)],
                                     out[RING][0:META, :]).then_inc(stored[RING], 16)
                    if done + 1 < NCH:
                        sp.wait_ge(w_high, (done + 1) * KB + START)
                        sp.wait_ge(w_low, (done + 1) * KB + START)
                        load(b0 + (i + 1) * CB)
                    for tile in range(NT):
                        r = tile % RING
                        sp.wait_ge(acc_freed[r], done * PER + (tile // RING + 1) + START)
                        row = META + tile * P if with_meta else tile * P
                        sp.dma_start(scratch[kind][row:row + P, bass.ds(i * W, W)],
                                     out[r][:, :]).then_inc(stored[r], 16)
            for r in range(RING):
                sp.wait_ge(stored[r], 16 * NCH * PER + START)
            sp.wait_ge(stored[RING], 16 * NCH + START)

        @block.gpsimd
        def _(pool):
            nc.gpsimd.memset(ident[:, :], 0.0).then_inc(ident_zero, 1)
            pool.wait_ge(ident_zero, START + 1)
            nc.gpsimd.affine_select(out=ident[:, :], in_=ident[:, :], compare_op=ALU.not_equal, fill=1.0,
                                    base=0, pattern=[[-1, HEADS]], channel_multiplier=1).then_inc(ident_ready, 1)
            pool.wait_ge(small_loaded, START + 32)
            nc.gpsimd.tensor_copy(wd_hi[:, :, :], wd[:, :, :]).then_inc(wd_split, 1)
            pool.wait_ge(wd_split, START + 1)
            nc.gpsimd.tensor_tensor(wd_lo[:, :, :], wd[:, :, :], wd_hi[:, :, :].bitcast(F32),
                                    ALU.subtract).then_inc(wd_split, 1)

        @block.tensor
        def _(pe):
            pe.wait_ge(wd_split, START + 2)
            pe.wait_ge(ident_ready, START + 1)

            def steps(c):
                t0, tn = CHUNKS[c]
                if c >= 2:
                    pe.wait_ge(dx_ready, c - 1 + START)
                for k in range(KB):
                    for w, u in ((wd_hi, ut_hi), (wd_hi, ut_lo), (wd_lo, ut_hi)):
                        last = nc.tensor.matmul(dacc[c % 2][0:HEADS, 0:tn], w[:, k, :], u[:, k, t0:t0 + tn],
                                                start=(k == 0 and u is ut_hi and w is wd_hi),
                                                stop=(k == KB - 1 and w is wd_lo))
                last.then_inc(dacc_ready, 1)

            def turn(c):
                tn = CHUNKS[c][1]
                pe.wait_ge(dta_ready, c + 1 + START)
                if c:
                    pe.wait_ge(dt_kept, c + START)
                tiles = max(tn // P, 1)
                rows = min(tn, P)
                for q in range(tiles):
                    for half, row in enumerate((dt_row, dta_row)):
                        last = nc.tensor.transpose(dtp[0:rows, q, half, :], row[:, q * P:q * P + rows], ident[:, :])
                last.then_inc(dt_turned, 1)

            steps(0)
            for c in range(len(CHUNKS)):
                if c + 1 < len(CHUNKS):
                    steps(c + 1)
                if c < len(CHUNKS) - 1:
                    turn(c)
            for n, (kind, _, with_meta) in enumerate(KINDS):
                for i in range(NCH):
                    done = i + n * NCH
                    tiles = ([(RING, 0, META, i)] if with_meta else []) + [
                        (t % RING, META + t * P, P, done * PER + t // RING) for t in range(NT)]
                    for at, (r, t0, tn, uses) in enumerate(tiles):
                        pe.wait_ge(acc_freed[r], uses + START)
                        for k in range(KB):
                            if at == 0:
                                pe.wait_ge(w_high, done * KB + (k + 1) + START)
                                pe.wait_ge(w_low, done * KB + (k + 1) + START)
                            for u, w in ((ut_hi, w_hi), (ut_hi, w_lo), (ut_lo, w_hi)):
                                last = nc.tensor.matmul(acc[r][0:tn, :], u[:, k, t0:t0 + tn], w[:, :, k, :],
                                                        start=(k == 0 and u is ut_hi and w is w_hi),
                                                        stop=(k == KB - 1 and u is ut_lo))
                            if at == len(tiles) - 1 and k < KB - 1:
                                last.then_inc(w_used, 1)
                        last.then_inc(acc_ready[r], 1)
            turn(len(CHUNKS) - 1)

        def each_chunk(eng, take):
            for n, (kind, _, with_meta) in enumerate(KINDS):
                for i in range(NCH):
                    take(i + n * NCH, i, kind, with_meta)

        @block.scalar
        def _(act):
            act.wait_ge(small_loaded, START + 32)
            nc.scalar.activation(rate[:, 0:1], dtc[:, 1:2], ACT.Exp).then_inc(rate_step, 1)
            for c, (t0, tn) in enumerate(CHUNKS):
                act.wait_ge(dacc_ready, c + 1 + START)
                if c:
                    act.wait_ge(dt_ready, c + START)
                nc.scalar.activation(dx[:, 0:tn], dacc[c % 2][0:HEADS, 0:tn], ACT.Identity,
                                     bias=dtc[:, 0:1]).then_inc(dx_ready, 1)
                act.wait_ge(da_ready, c + 1 + START)
                nc.scalar.activation(de[:, 0:tn], da[:, 0:tn], ACT.Exp).then_inc(de_ready, 1)
                act.wait_ge(de_ready, c + 1 + START)
                nc.scalar.activation(dl[:, 0:tn], de[:, 0:tn], ACT.Ln, bias=1.0).then_inc(dl_ready, 1)

            def high(done):
                act.wait_ge(w_loaded, done * 16 + 16 + START)
                for k in range(KB):
                    if done:
                        if k < KB - 1:
                            act.wait_ge(w_used, (done - 1) * (KB - 1) + (k + 1) + START)
                        else:
                            act.wait_ge(acc_ready[(NT - 1) % RING], done * PER + START)
                    nc.scalar.activation(w_hi[:, :, k, :], stage[:, :, k, :], ACT.Copy).then_inc(w_high, 1)

            def take(done, i, kind, with_meta):
                if done == 0:
                    high(0)
                if with_meta:
                    act.wait_ge(acc_ready[RING], i + 1 + START)
                    act.wait_ge(stored[RING], i * 16 + START)
                    nc.scalar.activation(out[RING][0:META, :], acc[RING][0:META, :],
                                         ACT.Copy).then_inc(acc_freed[RING], 1)
                for t in range(NT):
                    r = t % RING
                    if t == NT - 1 and done + 1 < NCH:
                        high(done + 1)
                    act.wait_ge(acc_ready[r], done * PER + (t // RING + 1) + START)
                    act.wait_ge(stored[r], (done * PER + t // RING) * 16 + START)
                    nc.scalar.activation(out[r][:, :], acc[r][:, :],
                                         ACT.Copy).then_inc(acc_freed[r], 1)

            each_chunk(act, take)

        @block.vector
        def _(dve):
            def keep(c):
                dve.wait_ge(dt_turned, c + 1 + START)
                if c == 0:
                    nc.vector.tensor_copy(dt_tok[0:META, 0, :, :], dtp[0:META, 0, :, :]).then_inc(dt_kept, 1)
                else:
                    q0 = 1 + (c - 1) * CB
                    nc.vector.tensor_copy(dt_tok[:, q0:q0 + CB, :, :], dtp[:, :, :, :]).then_inc(dt_kept, 1)

            dve.wait_ge(rate_step, START + 1)
            nc.vector.tensor_scalar(rate[:, 1:2], rate[:, 0:1], -1.0, None, ALU.mult).then_inc(rate_step, 1)
            for c, (t0, tn) in enumerate(CHUNKS):
                dve.wait_ge(dx_ready, c + 1 + START)
                if c:
                    dve.wait_ge(de_ready, c + START)
                nc.vector.scalar_tensor_tensor(out=da[:, 0:tn], in0=dx[:, 0:tn], scalar=-1.0, in1=dx[:, 0:tn],
                                               op0=ALU.mult, op1=ALU.min).then_inc(da_ready, 1)
                dve.wait_ge(dl_ready, c + 1 + START)
                if c:
                    dve.wait_ge(dt_turned, c + START)
                nc.vector.scalar_tensor_tensor(out=dt_row[:, 0:tn], in0=dx[:, 0:tn], scalar=0.0, in1=dl[:, 0:tn],
                                               op0=ALU.max, op1=ALU.add).then_inc(dt_ready, 1)
                dve.wait_ge(dt_ready, c + 1 + START)
                dve.wait_ge(rate_step, START + 2)
                nc.vector.tensor_scalar(dta_row[:, 0:tn], dt_row[:, 0:tn], rate[:, 1:2], None,
                                        ALU.mult).then_inc(dta_ready, 1)
                if c < len(CHUNKS) - 1:
                    keep(c)

            def take(done, i, kind, with_meta):
                for k in range(KB):
                    dve.wait_ge(w_high, done * KB + (k + 1) + START)
                    nc.vector.tensor_tensor(w_lo[:, :, k, :], stage[:, :, k, :], w_hi[:, :, k, :].bitcast(F32),
                                            ALU.subtract).then_inc(w_low, 1)

            each_chunk(dve, take)
            keep(len(CHUNKS) - 1)


def over_heads(columns, n):
    return columns.unsqueeze(2).to_broadcast([columns.shape[0], columns.shape[1], n])


def triangles(nc, pool, upper, later, zeroed, ready):
    for tile in (upper, later):
        nc.gpsimd.memset(tile[:, :], 1.0).then_inc(zeroed, 1)
    pool.wait_ge(zeroed, START + 2)
    nc.gpsimd.affine_select(out=upper[:, :], in_=upper[:, :], compare_op=ALU.is_ge, fill=0.0, base=0,
                            pattern=[[1, P]], channel_multiplier=-1).then_inc(ready, 1)
    nc.gpsimd.affine_select(out=later[:, :], in_=later[:, :], compare_op=ALU.is_gt, fill=0.0, base=0,
                            pattern=[[-1, P]], channel_multiplier=1).then_inc(ready, 1)


def scan_start(nc, scratch, dt_tok, state):
    with ExitStack() as ctx:
        m = Memory(nc, ctx)
        xc = m.sbuf("s0_xc", [P, KB + GROUPS, META])
        ident = m.sbuf("s0_ident", [P, P])
        ones, later = m.sbuf("s0_ones", [META, META]), m.sbuf("s0_later", [META, META])
        b_tok = m.sbuf("s0_b", [META, GROUPS, STATE])
        decay = m.sbuf("s0_decay", [META, HEADS])
        xdt, xde = m.sbuf("s0_xdt", [META, D]), m.sbuf("s0_xde", [META, D])
        px = m.psum("s0_px", [META, KB, P])
        pb = m.psum("s0_pb", [META, GROUPS, P])
        pd = m.psum("s0_pd", [META, HEADS])
        ps = m.psum("s0_ps", [P, GROUPS, W])
        loaded, made, ready = m.sem("s0_loaded"), m.sem("s0_made"), m.sem("s0_ready")
        turned, decay_ready, b_ready, xdt_ready, xde_ready = (m.sem(f"s0_{n}") for n in (
            "turned", "decay_ready", "b_ready", "xdt_ready", "xde_ready"))
        summed, state_ready = m.sem("s0_summed"), m.sem("s0_state_ready")
        m.start()
        block = ctx.enter_context(nc.Block())

        @block.sync
        def _(sp):
            sp.dma_start(xc[:, :, :], scratch["xbc"][0:KB + GROUPS, :, 0:META]
                         .rearrange("b p t -> p b t")).then_inc(loaded, 16)

        @block.gpsimd
        def _(pool):
            nc.gpsimd.memset(ident[:, :], 0.0).then_inc(made, 1)
            nc.gpsimd.memset(ones[:, :], 1.0).then_inc(made, 1)
            pool.wait_ge(made, START + 2)
            nc.gpsimd.affine_select(out=ident[:, :], in_=ident[:, :], compare_op=ALU.not_equal, fill=1.0,
                                    base=0, pattern=[[-1, P]], channel_multiplier=1).then_inc(ready, 1)
            nc.gpsimd.affine_select(out=later[:, :], in_=ones[:, :], compare_op=ALU.is_gt, fill=0.0, base=0,
                                    pattern=[[-1, META]], channel_multiplier=1).then_inc(ready, 1)

        @block.tensor
        def _(pe):
            pe.wait_ge(ready, START + 2)
            pe.wait_ge(loaded, START + 16)
            for b in range(KB):
                nc.tensor.transpose(px[:, b, :], xc[:, b, :], ident[:, :])
            for g in range(GROUPS):
                nc.tensor.transpose(pb[:, g, :], xc[:, KB + g, :], ident[:, :])
            nc.tensor.matmul(pd[:, :], later[:, :], dt_tok[0:META, 0, 1, :], start=True, stop=True).then_inc(turned, 1)
            pe.wait_ge(b_ready, START + 1)
            pe.wait_ge(xde_ready, START + 1)
            for g in range(GROUPS):
                last = nc.tensor.matmul(ps[:, g, :], b_tok[:, g, :], xde[:, g * W:(g + 1) * W], start=True, stop=True)
            last.then_inc(summed, 1)

        @block.scalar
        def _(act):
            act.wait_ge(turned, START + 1)
            nc.scalar.activation(decay[:, :], pd[:, :], ACT.Exp).then_inc(decay_ready, 1)
            nc.scalar.activation(b_tok[:, :, :], pb[:, :, :], ACT.Copy).then_inc(b_ready, 1)

        @block.vector
        def _(dve):
            dve.wait_ge(turned, START + 1)
            nc.vector.tensor_tensor(xdt[:, :].rearrange("p (h c) -> p h c", h=HEADS),
                                    px[:, :, :].rearrange("p b (h c) -> p (b h) c", h=2),
                                    over_heads(dt_tok[0:META, 0, 0, :], HEAD), ALU.mult).then_inc(xdt_ready, 1)
            dve.wait_ge(xdt_ready, START + 1)
            dve.wait_ge(decay_ready, START + 1)
            nc.vector.tensor_tensor(xde[:, :].rearrange("p (h c) -> p h c", h=HEADS),
                                    xdt[:, :].rearrange("p (h c) -> p h c", h=HEADS),
                                    over_heads(decay[:, :], HEAD), ALU.mult).then_inc(xde_ready, 1)
            dve.wait_ge(summed, START + 1)
            nc.vector.tensor_copy(state[:, :, :], ps[:, :, :]).then_inc(state_ready, 1)


def scan_stage(nc, scratch, d_cols, dt_tok, state):
    with ExitStack() as ctx:
        m = Memory(nc, ctx)
        GB = KB // GROUPS
        upper, later, ones = m.sbuf("s_upper", [P, P]), m.sbuf("s_later", [P, P]), m.sbuf("s_ones", [P, P])
        ident = m.sbuf("s_ident", [P, P])
        d_col = m.sbuf("s_d_col", [P, KB])
        xc = [m.sbuf(f"s_xc{s}", [P, XB, P]) for s in range(2)]
        zt = [m.sbuf(f"s_zt{s}", [P, KB, P]) for s in range(2)]
        b_tok = [m.sbuf(f"s_b{s}", [P, GROUPS, STATE]) for s in range(2)]
        expo = [m.sbuf(f"s_expo{s}", [P, 3, HEADS]) for s in range(2)]
        cbm = [m.sbuf(f"s_cbm{s}", [P, GROUPS, P]) for s in range(2)]
        ua = [m.sbuf(f"s_ua{g}", [P, HPG, P]) for g in range(GROUPS)]
        decay = [m.sbuf(f"s_decay{g}", [P, HPG, P]) for g in range(GROUPS)]
        mt = [m.sbuf(f"s_mt{g}", [P, HPG, P]) for g in range(GROUPS)]
        xdt = [m.sbuf(f"s_xdt{g}", [P, W]) for g in range(GROUPS)]
        xde = [m.sbuf(f"s_xde{g}", [P, W]) for g in range(GROUPS)]
        yo = [m.sbuf(f"s_yo{g}", [P, W]) for g in range(GROUPS)]
        ysum = [m.sbuf(f"s_ysum{g}", [P, W]) for g in range(GROUPS)]
        xd = [m.sbuf(f"s_xd{g}", [P, GB, P]) for g in range(GROUPS)]
        yt = [m.sbuf(f"s_yt{g}", [P, GB, P]) for g in range(GROUPS)]
        gated = [m.sbuf(f"s_gated{g}", [P, GB, P]) for g in range(GROUPS)]
        px = m.psum("s_px", [P, GB, P])
        pbc = m.psum("s_pbc", [P, 2 * GROUPS, P])
        pc = m.psum("s_pc", [P, 3, HEADS])
        pseg = m.psum("s_pseg", [P, HPG, P])
        pyo, pyd, pst = m.psum("s_pyo", [P, W]), m.psum("s_pyd", [P, W]), m.psum("s_pst", [P, W])

        def per_unit(name):
            return [m.sems(f"{name}{s}", GROUPS) for s in range(2)]

        d_loaded, filled, made = m.sem("d_loaded"), m.sem("s_filled"), m.sem("s_made")
        xc_loaded, zt_loaded = m.sems("xc_loaded", 2), m.sems("zt_loaded", 2)
        bc_ready, sums_ready = m.sems("bc_ready", 2), m.sems("sums_ready", 2)
        b_ready, expo_ready, cbm_ready = m.sems("b_ready", 2), m.sems("expo_ready", 2), m.sems("cbm_ready", 2)
        x_turned, ua_ready, seg_ready, decay_ready = (per_unit(n) for n in ("x_turned", "ua_ready", "seg_ready", "decay_ready"))
        xdt_ready, xde_ready, m_ready = (per_unit(n) for n in ("xdt_ready", "xde_ready", "m_ready"))
        off_done, st_done, diag_done = (per_unit(n) for n in ("off_done", "st_done", "diag_done"))
        yo_ready, decayed, state_ready, ysum_ready = (per_unit(n) for n in ("yo_ready", "decayed", "state_ready", "ysum_ready"))
        y_turned, xd_ready, yt_ready, gated_ready = (per_unit(n) for n in ("y_turned", "xd_ready", "yt_ready", "gated_ready"))
        stored = m.sems("s_stored", GROUPS)
        m.start()
        block = ctx.enter_context(nc.Block())
        PAIRS_OF_CHUNKS = NT // 2

        def before(s, g, i):
            return (s, 0, i + 1) if g else (1 - s, 1, i + s)

        def dt_of(i, s, which, g):
            if isinstance(i, int):
                return dt_tok[:, 1 + 2 * i + s, which, g * HPG:(g + 1) * HPG]
            return dt_tok[:, bass.ds(i * 2 + (1 + s), 1), which, g * HPG:(g + 1) * HPG].rearrange("p o h -> p (o h)")

        def pipeline(eng, *stages):
            EACH = 2 * GROUPS
            LAST = PAIRS_OF_CHUNKS - 1

            def step(i, j):
                for ahead, do in stages:
                    shift, unit = (j + ahead) // EACH, (j + ahead) % EACH
                    at = i + shift if shift else i
                    if not isinstance(at, int) or 0 <= at <= LAST:
                        do(unit // GROUPS, unit % GROUPS, at)

            for j in range(-2, EACH):
                step(0, j)
            with eng.Fori(1, LAST) as i:
                for j in range(EACH):
                    step(i, j)
            for j in range(EACH + 1):
                step(LAST, j)

        @block.sync
        def _(sp):
            sp.dma_start(d_col[:, :], d_cols).then_inc(d_loaded, 16)

            def load_xc(s, i):
                sp.dma_start(xc[s][:, :, :], scratch["xbc"][:, :, bass.ds(i * (2 * P) + (s * P + META), P)]
                             .rearrange("b p t -> p b t")).then_inc(xc_loaded[s], 16)

            def load_zt(s, i):
                sp.dma_start(zt[s][:, :, :], scratch["gate"][KB:MB, :, bass.ds(i * (2 * P) + s * P, P)]
                             .rearrange("b p t -> p b t")).then_inc(zt_loaded[s], 16)

            def store(s, g, i):
                sp.wait_ge(gated_ready[s][g], i + 1 + START)
                sp.dma_start(scratch["mixed"][KB + g * GB:KB + (g + 1) * GB, :, bass.ds(i * (2 * P) + s * P, P)]
                             .rearrange("b p t -> p b t"), gated[g][:, :, :]).then_inc(stored[g], 16)

            def step(i, more):
                for s in range(2):
                    store(s, 0, i)
                    if more:
                        sp.wait_ge(off_done[s][1], i + 1 + START)
                        sp.wait_ge(xd_ready[s][1], i + 1 + START)
                        load_xc(s, i + 1)
                    store(s, 1, i)
                    if more:
                        load_zt(s, i + 1)

            for s in range(2):
                load_xc(s, 0)
            for s in range(2):
                load_zt(s, 0)
            with sp.Fori(0, PAIRS_OF_CHUNKS - 1) as i:
                step(i, True)
            step(PAIRS_OF_CHUNKS - 1, False)
            for g in range(GROUPS):
                sp.wait_ge(stored[g], 16 * NT + START)

        @block.gpsimd
        def _(pool):
            triangles(nc, pool, upper, later, filled, made)
            nc.gpsimd.memset(ones[:, :], 1.0).then_inc(made, 1)
            nc.gpsimd.memset(ident[:, :], 0.0).then_inc(filled, 1)
            pool.wait_ge(filled, START + 3)
            nc.gpsimd.affine_select(out=ident[:, :], in_=ident[:, :], compare_op=ALU.not_equal, fill=1.0,
                                    base=0, pattern=[[-1, P]], channel_multiplier=1).then_inc(made, 1)
            pool.wait_ge(made, START + 4)
            pool.wait_ge(d_loaded, START + 16)

            def spread_steps(s, g, i):
                pool.wait_ge(seg_ready[1 - s][g], i + s + START)
                nc.gpsimd.tensor_tensor(ua[g][:, :, :], upper[:, :].unsqueeze(1).to_broadcast([P, HPG, P]),
                                        over_heads(dt_of(i, s, 1, g), P), ALU.mult).then_inc(ua_ready[s][g], 1)

            def skip(s, g, i):
                pool.wait_ge(xc_loaded[s], i * 16 + 16 + START)
                pool.wait_ge(yt_ready[1 - s][g], i + s + START)
                nc.gpsimd.tensor_tensor(xd[g][:, :, :], xc[s][:, g * GB:(g + 1) * GB, :],
                                        spread(d_col[:, g * GB:(g + 1) * GB], P), ALU.mult).then_inc(xd_ready[s][g], 1)

            def gate(s, g, i):
                pool.wait_ge(zt_loaded[s], i * 16 + 16 + START)
                pool.wait_ge(yt_ready[s][g], i + 1 + START)
                pool.wait_ge(stored[g], i * 32 + 16 * s + START)
                nc.gpsimd.tensor_tensor(gated[g][:, :, :], yt[g][:, :, :], zt[s][:, g * GB:(g + 1) * GB, :],
                                        ALU.mult).then_inc(gated_ready[s][g], 1)

            pipeline(pool, (2, spread_steps), (1, skip), (-1, gate))

        @block.tensor
        def _(pe):
            pe.wait_ge(made, START + 4)

            def front(s, g, i):
                if g == 0:
                    pe.wait_ge(xc_loaded[s], i * 16 + 16 + START)
                    pe.wait_ge(b_ready[1 - s], i + s + START)
                    pe.wait_ge(cbm_ready[1 - s], i + s + START)
                    for q in range(GROUPS):
                        nc.tensor.transpose(pbc[:, q, :], xc[s][:, KB + q, :], ident[:, :])
                    for q in range(GROUPS):
                        last = nc.tensor.matmul(pbc[:, GROUPS + q, :], xc[s][:, KB + q, :], xc[s][:, KB + GROUPS + q, :],
                                                start=True, stop=True)
                    last.then_inc(bc_ready[s], 1)
                    pe.wait_ge(expo_ready[1 - s], i + s + START)
                    for n, lhs in enumerate((upper, later, ones)):
                        rhs = (dt_tok[:, 1 + 2 * i + s, 1, :] if isinstance(i, int) else
                               dt_tok[:, bass.ds(i * 2 + (1 + s), 1), 1, :].rearrange("p o h -> p (o h)"))
                        last = nc.tensor.matmul(pc[:, n, :], lhs[:, :], rhs, start=True, stop=True)
                    last.then_inc(sums_ready[s], 1)
                ps, pg, count = before(s, g, i)
                pe.wait_ge(xdt_ready[ps][pg], count + START)
                for b in range(GB):
                    last = nc.tensor.transpose(px[:, b, :], xc[s][:, g * GB + b, :], ident[:, :])
                last.then_inc(x_turned[s][g], 1)
                pe.wait_ge(ua_ready[s][g], i + 1 + START)
                pe.wait_ge(decay_ready[ps][pg], count + START)
                for half in range(2):
                    hs = slice(half * (HPG // 2), (half + 1) * (HPG // 2))
                    last = nc.tensor.matmul(pseg[:, hs, :], later[:, :], ua[g][:, hs, :], start=True, stop=True)
                last.then_inc(seg_ready[s][g], 1)

            def turn(s, g, i):
                pe.wait_ge(ysum_ready[s][g], i + 1 + START)
                for b in range(GB):
                    last = nc.tensor.transpose(pyd[:, b * P:(b + 1) * P], ysum[g][:, b * P:(b + 1) * P], ident[:, :])
                last.then_inc(y_turned[s][g], 1)

            def multiply(s, g, i):
                ps, pg, count = before(s, g, i)
                pe.wait_ge(state_ready[1 - s][g], i + s + START)
                pe.wait_ge(yo_ready[ps][pg], count + START)
                nc.tensor.matmul(pyo[:, :], xc[s][:, KB + GROUPS + g, :], state[:, g, :],
                                 start=True, stop=True).then_inc(off_done[s][g], 1)
                pe.wait_ge(b_ready[s], i + 1 + START)
                pe.wait_ge(xde_ready[s][g], i + 1 + START)
                pe.wait_ge(state_ready[ps][pg], count + START)
                nc.tensor.matmul(pst[:, :], b_tok[s][:, g, :], xde[g][:, :], start=True, stop=True).then_inc(st_done[s][g], 1)
                pe.wait_ge(m_ready[s][g], i + 1 + START)
                pe.wait_ge(yt_ready[ps][pg], count + START)
                for h in range(HPG):
                    last = nc.tensor.matmul(pyd[:, h * HEAD:(h + 1) * HEAD], mt[g][:, h, :],
                                            xdt[g][:, h * HEAD:(h + 1) * HEAD], start=True, stop=True)
                last.then_inc(diag_done[s][g], 1)

            pipeline(pe, (1, front), (-1, turn), (0, multiply))

        @block.scalar
        def _(act):
            def front(s, g, i):
                if g == 0:
                    act.wait_ge(bc_ready[s], i + 1 + START)
                    act.wait_ge(st_done[s][1], i + START)
                    nc.scalar.activation(b_tok[s][:, :, :], pbc[:, 0:GROUPS, :], ACT.Copy).then_inc(b_ready[s], 1)
                    act.wait_ge(sums_ready[s], i + 1 + START)
                    act.wait_ge(decayed[s][1], i + START)
                    nc.scalar.activation(expo[s][:, :, :], pc[:, :, :], ACT.Exp).then_inc(expo_ready[s], 1)
                act.wait_ge(seg_ready[s][g], i + 1 + START)
                act.wait_ge(m_ready[1 - s][g], i + s + START)
                nc.scalar.activation(decay[g][:, :, :], pseg[:, :, :], ACT.Exp).then_inc(decay_ready[s][g], 1)

            pipeline(act, (1, front))

        @block.vector
        def _(dve):
            dve.wait_ge(made, START + 4)

            def heads(tile):
                return tile[:, :].rearrange("p (h c) -> p h c", h=HPG)

            def inputs(s, g, i):
                hs = slice(g * HPG, (g + 1) * HPG)
                if g == 0:
                    dve.wait_ge(bc_ready[s], i + 1 + START)
                    dve.wait_ge(b_ready[s], i + 1 + START)
                    nc.vector.tensor_tensor(cbm[s][:, :, :], pbc[:, GROUPS:2 * GROUPS, :],
                                            upper[:, :].unsqueeze(1).to_broadcast([P, GROUPS, P]),
                                            ALU.mult).then_inc(cbm_ready[s], 1)
                dve.wait_ge(x_turned[s][g], i + 1 + START)
                dve.wait_ge(diag_done[1 - s][g], i + s + START)
                nc.vector.tensor_tensor(heads(xdt[g]), px[:, :, :].rearrange("p b (h c) -> p (b h) c", h=2),
                                        over_heads(dt_of(i, s, 0, g), HEAD), ALU.mult).then_inc(xdt_ready[s][g], 1)
                dve.wait_ge(xdt_ready[s][g], i + 1 + START)
                dve.wait_ge(expo_ready[s], i + 1 + START)
                dve.wait_ge(st_done[1 - s][g], i + s + START)
                nc.vector.tensor_tensor(heads(xde[g]), heads(xdt[g]), over_heads(expo[s][:, 1, hs], HEAD),
                                        ALU.mult).then_inc(xde_ready[s][g], 1)

            def weights(s, g, i):
                dve.wait_ge(decay_ready[s][g], i + 1 + START)
                dve.wait_ge(cbm_ready[s], i + 1 + START)
                nc.vector.tensor_tensor(mt[g][:, :, :], decay[g][:, :, :],
                                        cbm[s][:, g, :].unsqueeze(1).to_broadcast([P, HPG, P]),
                                        ALU.mult).then_inc(m_ready[s][g], 1)

            def states(s, g, i):
                hs = slice(g * HPG, (g + 1) * HPG)
                dve.wait_ge(off_done[s][g], i + 1 + START)
                nc.vector.tensor_tensor(heads(yo[g]), heads(pyo), over_heads(expo[s][:, 0, hs], HEAD),
                                        ALU.mult).then_inc(yo_ready[s][g], 1)
                own = state[:, g, :].rearrange("p (h c) -> p h c", h=HPG)
                nc.vector.tensor_tensor(own, own, over_heads(expo[s][:, 2, hs], HEAD), ALU.mult).then_inc(decayed[s][g], 1)
                dve.wait_ge(decayed[s][g], i + 1 + START)
                dve.wait_ge(st_done[s][g], i + 1 + START)
                nc.vector.tensor_tensor(state[:, g, :], state[:, g, :], pst[:, :], ALU.add).then_inc(state_ready[s][g], 1)

            def sum_y(s, g, i):
                dve.wait_ge(diag_done[s][g], i + 1 + START)
                dve.wait_ge(yo_ready[s][g], i + 1 + START)
                dve.wait_ge(y_turned[1 - s][g], i + s + START)
                nc.vector.tensor_tensor(ysum[g][:, :], yo[g][:, :], pyd[:, :], ALU.add).then_inc(ysum_ready[s][g], 1)

            def add_skip(s, g, i):
                dve.wait_ge(y_turned[s][g], i + 1 + START)
                dve.wait_ge(xd_ready[s][g], i + 1 + START)
                dve.wait_ge(gated_ready[1 - s][g], i + s + START)
                nc.vector.tensor_tensor(yt[g][:, :, :], xd[g][:, :, :], pyd[:, :].rearrange("p (b c) -> p b c", b=GB),
                                        ALU.add).then_inc(yt_ready[s][g], 1)

            pipeline(dve, (1, inputs), (-1, add_skip), (0, states), (1, weights), (0, sum_y))


def key_block(kb):
    return (0, META) if kb == 0 else (META + (kb - 1) * P, P)


def attention_units():
    units = []
    for c in range(NW):
        prev = None
        for kb in range((c + 1) * (W // P), -1, -1):
            start = max(kb - 1 - c * (W // P), 0) * P if kb else 0
            units.append((c, kb, start, prev))
            prev = start
    return units


def attention_stage(nc, scratch):
    UNITS = attention_units()
    U = len(UNITS)
    N = 2 * U
    C = 2 * NW
    ITER = PAIRS // 2
    RING = 3
    FIRST = META + W

    def unit(n):
        return UNITS[n % U]

    def diagonal(n):
        c, kb, _, _ = unit(n)
        return kb > c * (W // P)

    def first(n):
        return unit(n)[3] is None

    def last(n):
        return unit(n)[1] == 0

    def rows(n):
        return key_block(unit(n)[1])[1]

    def bank(n):
        return n % N % RING

    def bank_before(n):
        return next(x for x in range(n - 1, n - 2 * RING, -1) if bank(x % N) == bank(n))

    def having(test, n):
        return sum(test(x) for x in range(n)) if n >= 0 else -sum(test(x % N) for x in range(n, 0))

    def carried(n):
        return not first(n)

    def chunk_of(n):
        return n // U * NW + unit(n)[0]

    CARRIED = having(carried, N)

    with ExitStack() as ctx:
        m = Memory(nc, ctx)

        def ring(name, n, dt=F32, shape=(P, 2, W)):
            return [m.sbuf(f"a_{name}{r}", list(shape), dt) for r in range(n)]

        k_high, k_low = ring("k_high", 2, F32R, (P, 2, T)), ring("k_low", 2, F32R, (P, 2, T))
        v = ring("v", 2, F32, (P, NT + 1, P))
        q = ring("q", 2, F32R)
        gate = ring("gate", 2, F32, (P, W))
        out = ring("out", 2, F32, (P, W))
        soft = ring("soft", RING)
        sp_ = ring("sp", RING)
        sp_hi, sp_lo = ring("sp_hi", RING, F32R), ring("sp_lo", RING, F32R)
        newer = ring("newer", RING)
        w = ring("w", RING)
        plain = m.sbuf("a_plain", [P, 2, P])
        minus = m.sbuf("a_minus", [P, P], F32R)
        ident = m.sbuf("a_ident", [P, P], BF16)
        never = m.sbuf("a_never", [P, P], BF16)
        zero = m.sbuf("a_zero", [P, 1])
        z = [m.psum(f"a_z{r}", [P, 2, W]) for r in range(RING)]
        o = [m.psum(f"a_o{r}", [P, W]) for r in range(2)]

        filled, made, minus_ready = m.sem("a_filled"), m.sem("a_made"), m.sem("minus_ready")
        k_loaded = [m.sems(f"k_loaded{slot}", 2) for slot in range(2)]
        v_loaded = [m.sems(f"v_loaded{slot}", 2) for slot in range(2)]
        q_loaded, gate_loaded = m.sems("q_loaded", 2), m.sems("gate_loaded", 2)
        stored = m.sems("a_stored", 2)
        COUNTERS = ("z_ready", "exp_ready", "capped", "ln_ready", "sp_ready", "high_ready", "low_ready", "newer_ready",
                    "summed_0", "summed", "w_0_ready", "w_ready", "applied", "out_ready")
        count = {name: m.sem(name) for name in COUNTERS}

        m.start()
        block = ctx.enter_context(nc.Block())

        def await_units(eng, name, it, n, total=N):
            eng.wait_ge(count[name], it * total + (n + START))

        def done(name, instruction):
            instruction.then_inc(count[name], 1)

        def columns(tile, n, lo=None, hi=W):
            return tile[0:rows(n), :, (unit(n)[2] if lo is None else lo):hi]

        @block.sync
        def _(sp):
            def load_pair(slot, it, part):
                pair = it * 2 + slot
                one = lambda name: scratch[name][bass.ds(pair, 1), :, :].rearrange("b (h p) t -> p (b h) t", h=2)
                if part == 0:
                    sp.dma_start(v[slot][0:META, 0, :],
                                 scratch["v"][0:META, bass.ds(pair * P, P)]).then_inc(v_loaded[slot][0], 16)
                t0, t1 = ((0, FIRST), (FIRST, T))[part]
                b0, b1 = 1 + max(t0 - META, 0) // P, 1 + (t1 - META) // P
                for tile, name in ((k_high, "k_hi"), (k_low, "k_lo")):
                    for half in range(2):
                        sp.dma_start(tile[slot][half * HEAD:(half + 1) * HEAD, :, t0:t1].bitcast(F32),
                                     one(name)[:, :, t0:t1]).then_inc(k_loaded[slot][part], 16)
                sp.dma_start(v[slot][:, b0:b1, :], scratch["v"][META + (b0 - 1) * P:t1, bass.ds(pair * P, P)]
                             .rearrange("(b p) c -> p b c", p=P)).then_inc(v_loaded[slot][part], 16)

            def load_chunk(ch, it):
                pair, c, r = it * 2 + ch // NW, ch % NW, ch % 2
                for half, name in enumerate(("q_hi", "q_lo")):
                    sp.dma_start(q[r][half * HEAD:(half + 1) * HEAD, :, :].bitcast(F32),
                                 scratch[name][bass.ds(pair, 1), :, c * W:(c + 1) * W]
                                 .rearrange("b (h p) t -> p (b h) t", h=2)).then_inc(q_loaded[r], 16)
                sp.dma_start(gate[r][:, :], scratch["gate"][bass.ds(pair, 1), :, c * W:(c + 1) * W]
                             .rearrange("b p t -> (b p) t")).then_inc(gate_loaded[r], 16)

            def step(it, more):
                for ch in range(C):
                    await_units(sp, "out_ready", it, ch + 1, C)
                    sp.dma_start(scratch["mixed"][bass.ds(it * 2 + ch // NW, 1), :, ch % NW * W:(ch % NW + 1) * W]
                                 .rearrange("b p t -> (b p) t"), out[ch % 2][:, :]).then_inc(stored[ch % 2], 16)
                    if ch + 2 < C:
                        load_chunk(ch + 2, it)
                    elif more:
                        load_chunk(ch + 2 - C, it + 1)
                    if ch % NW == NW - 1 and more:
                        for part in range(2):
                            load_pair(ch // NW, it + 1, part)

            load_chunk(0, 0)
            load_pair(0, 0, 0)
            load_chunk(1, 0)
            load_pair(0, 0, 1)
            for part in range(2):
                load_pair(1, 0, part)
            with sp.Fori(0, ITER - 1) as it:
                step(it, True)
            step(ITER - 1, False)
            for r in range(2):
                sp.wait_ge(stored[r], 16 * ITER * C // 2 + START)

        @block.tensor
        def _(pe):
            def scores(it, n):
                c, kb, start, _ = unit(n)
                slot, ch = n // U, chunk_of(n)
                if first(n):
                    pe.wait_ge(k_loaded[slot][ch % NW > 0], it * 64 + 64 + START)
                    pe.wait_ge(q_loaded[ch % 2], it * (32 * NW) + (ch // 2 + 1) * 32 + START)
                t0, tn = key_block(kb)
                for h, name in enumerate(("w_0_ready", "w_ready")):
                    await_units(pe, name, it, bank_before(n) + 1)
                    for part, k in enumerate((k_high, k_low)):
                        mm = nc.tensor.matmul(z[bank(n)][0:tn, h, start:W], k[slot][:, h, t0:t0 + tn],
                                              q[ch % 2][:, h, start:W], start=(part == 0), stop=(part == 1),
                                              skip_group_check=True)
                    if diagonal(n):
                        mm = nc.tensor.matmul(z[bank(n)][:, h, start:start + P], ident[:, :], never[:, :],
                                              start=False, stop=True, skip_group_check=True)
                done("z_ready", mm)

            def subtract_sums(it, n):
                _, kb, start, prev = unit(n)
                tn = rows(n)

                def add(h, lhs, tile, kk, lo):
                    return nc.tensor.matmul(z[bank(n)][0:tn, h, lo:W], lhs, tile[bank(n)][0:kk, h, lo:W],
                                            start=False, stop=True, skip_group_check=True)

                await_units(pe, "sp_ready", it, n + 1)
                if tn < P:
                    await_units(pe, "high_ready", it, n + 1)
                    await_units(pe, "low_ready", it, n + 1)
                if carried(n):
                    await_units(pe, "newer_ready", it, having(carried, n + 1), CARRIED)
                    for h in range(2):
                        add(h, plain[:, 1, 0:tn], newer, P, prev)
                for h, name in enumerate(("summed_0", "summed")):
                    if h == 0 and tn == P:
                        await_units(pe, "high_ready", it, n + 1)
                    add(h, minus[0:tn, :tn], sp_hi, tn, start)
                    if h == 0 and tn == P:
                        await_units(pe, "low_ready", it, n + 1)
                    done(name, add(h, minus[0:tn, :tn], sp_lo, tn, start))

            def apply(it, n):
                _, kb, start, _ = unit(n)
                slot, ch, tn = n // U, chunk_of(n), rows(n)
                if first(n):
                    loads = 16 if ch % NW else 32
                    pe.wait_ge(v_loaded[slot][ch % NW > 0], it * loads + loads + START)
                    await_units(pe, "out_ready", it, ch - 1, C)
                await_units(pe, "w_ready", it, n + 1)
                for h in range(2):
                    mm = nc.tensor.matmul(o[ch % 2][h * HEAD:(h + 1) * HEAD, start:W],
                                          v[slot][0:tn, kb, h * HEAD:(h + 1) * HEAD], w[bank(n)][0:tn, h, start:W],
                                          start=first(n), stop=last(n), skip_group_check=True)
                done("applied", mm)

            pe.wait_ge(minus_ready, START + 1)
            pe.wait_ge(made, START + 3)
            with pe.Fori(0, ITER) as it:
                for n in range(-RING, N + 1):
                    if 0 <= n < N:
                        subtract_sums(it, n)
                    if n >= 1:
                        apply(it, n - 1)
                    if n + RING < N:
                        scores(it, n + RING)

        @block.scalar
        def _(act):
            nc.scalar.preload_act_table_set(EXP_AND_LN)
            act.wait_ge(made, START + 3)
            nc.scalar.activation(minus[:, :], plain[:, 0, :], ACT.Copy).then_inc(minus_ready, 1)

            def exp_scores(it, n):
                await_units(act, "z_ready", it, n + 1)
                await_units(act, "sp_ready", it, bank_before(n) + 1)
                done("exp_ready", nc.scalar.activation(columns(soft[bank(n)], n), columns(z[bank(n)], n), ACT.Exp))

            def ln(it, n):
                await_units(act, "capped", it, n + 1)
                tile = columns(soft[bank(n)], n)
                done("ln_ready", nc.scalar.activation(tile, tile, ACT.Ln, bias=1.0))

            def weights(it, n):
                start, tn = unit(n)[2], rows(n)
                await_units(act, "applied", it, bank_before(n) + 1)
                for h, (sums, ready) in enumerate((("summed_0", "w_0_ready"), ("summed", "w_ready"))):
                    await_units(act, sums, it, n + 1)
                    done(ready, nc.scalar.activation(w[bank(n)][0:tn, h, start:W], z[bank(n)][0:tn, h, start:W],
                                                     ACT.Exp))

            with act.Fori(0, ITER) as it:
                for n in range(-2, N):
                    if 0 <= n + 1 < N:
                        ln(it, n + 1)
                    if n + 2 < N:
                        exp_scores(it, n + 2)
                    if n >= 0:
                        weights(it, n)

        @block.vector
        def _(dve):
            def cap(it, n):
                await_units(dve, "exp_ready", it, n + 1)
                tile = columns(soft[bank(n)], n)
                done("capped", nc.vector.tensor_scalar(tile, tile, LN_TOP, None, ALU.min))

            def softplus(it, n):
                await_units(dve, "ln_ready", it, n + 1)
                await_units(dve, "newer_ready", it, having(carried, bank_before(n) + 2), CARRIED)
                tile = sp_[bank(n)]
                mx = nc.vector.tensor_tensor(columns(tile, n), columns(soft[bank(n)], n), columns(z[bank(n)], n), ALU.max)
                done("sp_ready", mx)

            def split(it, n):
                await_units(dve, "sp_ready", it, n + 1)
                await_units(dve, "summed", it, bank_before(n) + 1)
                done("high_ready", nc.vector.tensor_copy(columns(sp_hi[bank(n)], n), columns(sp_[bank(n)], n)))
                await_units(dve, "high_ready", it, n + 1)
                done("low_ready", nc.vector.tensor_tensor(columns(sp_lo[bank(n)], n), columns(sp_[bank(n)], n),
                                                          columns(sp_hi[bank(n)], n).bitcast(F32), ALU.subtract))

            def gated(it, n):
                ch = chunk_of(n)
                await_units(dve, "applied", it, n + 1)
                dve.wait_ge(gate_loaded[ch % 2], it * (16 * NW) + (ch // 2 + 1) * 16 + START)
                dve.wait_ge(stored[ch % 2], it * (16 * NW) + ch // 2 * 16 + START)
                done("out_ready", nc.vector.tensor_tensor(out[ch % 2][:, :], gate[ch % 2][:, :], o[ch % 2][:, :], ALU.mult))

            with dve.Fori(0, ITER) as it:
                for n in range(-2, N + 2):
                    if 0 <= n + 1 < N:
                        softplus(it, n + 1)
                    if n + 2 < N:
                        cap(it, n + 2)
                    if 0 <= n + 1 < N:
                        split(it, n + 1)
                    if n >= 2 and last(n - 2):
                        gated(it, n - 2)

        @block.gpsimd
        def _(pool):
            nc.gpsimd.memset(plain[:, :, :], -1.0).then_inc(filled, 1)
            nc.gpsimd.memset(ident[:, :], 0.0).then_inc(filled, 1)
            nc.gpsimd.memset(never[:, :], 0.0).then_inc(filled, 1)
            nc.gpsimd.memset(zero[:, :], 0.0).then_inc(filled, 1)
            pool.wait_ge(filled, START + 4)
            nc.gpsimd.affine_select(out=plain[:, 0, :], in_=plain[:, 0, :], compare_op=ALU.is_ge, fill=0.0, base=0,
                                    pattern=[[-1, P]], channel_multiplier=1).then_inc(made, 1)
            nc.gpsimd.affine_select(out=ident[:, :], in_=ident[:, :], compare_op=ALU.not_equal, fill=1.0, base=0,
                                    pattern=[[-1, P]], channel_multiplier=1).then_inc(made, 1)
            nc.gpsimd.affine_select(out=never[:, :], in_=never[:, :], compare_op=ALU.is_gt, fill=NEVER, base=0,
                                    pattern=[[1, P]], channel_multiplier=-1).then_inc(made, 1)

            def sum_newer(it, n):
                new, old, add = newer[bank(n)], newer[bank(n - 1)], sp_[bank(n - 1)]
                prev, before = unit(n)[3], unit(n - 1)[3]
                await_units(pool, "sp_ready", it, n)
                await_units(pool, "summed", it, bank_before(n) + 1)
                await_units(pool, "newer_ready", it, having(carried, n), CARRIED)
                def taken(lo, hi):
                    return nc.gpsimd.tensor_tensor(new[:, :, lo:hi], add[:, :, lo:hi],
                                                   zero[:, :].unsqueeze(2).to_broadcast([P, 2, hi - lo]), ALU.add)

                if before is None:
                    mm = taken(prev, W)
                else:
                    if before > prev:
                        taken(prev, before)
                    mm = nc.gpsimd.tensor_tensor(new[:, :, before:W], old[:, :, before:W], add[:, :, before:W], ALU.add)
                done("newer_ready", mm)

            with pool.Fori(0, ITER) as it:
                for n in range(-1, N):
                    if n + 1 < N and carried(n + 1):
                        sum_newer(it, n + 1)


def output_stage(nc, scratch, x, w_out, group_w, final_w, out):
    with ExitStack() as ctx:
        m = Memory(nc, ctx)
        NH = D // W
        w_hi = m.sbuf("o_w_hi", [P, MB, D], F32R)
        w_lo = m.sbuf("o_w_lo", [P, MB, D], F32R)
        g = [m.sbuf(f"o_g{s}", [P, MB, P]) for s in range(2)]
        g_hi = [m.sbuf(f"o_g_hi{s}", [P, MB, P], F32R) for s in range(2)]
        g_lo = [m.sbuf(f"o_g_lo{s}", [P, MB, P], F32R) for s in range(2)]
        squares = m.sbuf("o_squares", [P, D])
        sq_sum = [m.sbuf(f"o_sq_sum{s}", [P, 2, P]) for s in range(2)]
        h = [m.sbuf(f"o_h{s}", [P, D]) for s in range(2)]
        y = [m.sbuf(f"o_y{s}", [P, D]) for s in range(2)]
        gw = m.sbuf("o_gw", [P, MB])
        fw = m.sbuf("o_fw", [P, D])
        ones, power = m.sbuf("o_ones", [P, 1]), m.sbuf("o_power", [P, 2])
        var = [m.sbuf(f"o_var{s}", [P, 2]) for s in range(2)]
        rstd = [m.sbuf(f"o_rstd{s}", [P, 2]) for s in range(2)]
        f_ssq = [m.sbuf(f"o_f_ssq{s}", [P, 1]) for s in range(2)]
        f_var = [m.sbuf(f"o_f_var{s}", [P, 1]) for s in range(2)]
        f_rstd = [m.sbuf(f"o_f_rstd{s}", [P, 1]) for s in range(2)]
        pss = m.psum("o_pss", [P, 2])
        acc = [[m.psum(f"o_acc{n}{q}", [P, W]) for q in range(2)] for n in range(NH)]

        made, gw_loaded, fw_loaded = m.sem("o_made"), m.sem("gw_loaded"), m.sem("fw_loaded")
        staging = y + h
        STAGES = len(staging)
        w_loaded, w_high, w_low = m.sems("o_w_loaded", STAGES), m.sem("o_w_high"), m.sem("o_w_low")
        g_loaded = [m.sems(f"g_loaded{s}", 2) for s in range(2)]
        h_loaded = m.sems("h_loaded", 2)
        squared = [m.sems(f"squared{s}", 2) for s in range(2)]
        reduced = [m.sems(f"reduced{s}", 2) for s in range(2)]
        weighed, g_high, g_low = m.sems("weighed", 2), m.sems("g_high", 2), m.sems("g_low", 2)
        ssq_ready, var_ready, rstd_ready = m.sems("o_ssq_ready", 2), m.sems("o_var_ready", 2), m.sems("o_rstd_ready", 2)
        acc_ready = [[m.sems(f"o_acc_ready{s}{n}", 2) for n in range(NH)] for s in range(2)]
        half_added = [m.sems(f"half_added{s}", NH) for s in range(2)]
        added = [m.sems(f"added{s}", NH) for s in range(2)]
        f_ssq_ready, f_var_ready, f_rstd_ready = (m.sems(n, 2) for n in ("f_ssq_ready", "f_var_ready", "f_rstd_ready"))
        y_ready, stored = m.sems("y_ready", 2), m.sems("o_stored", 2)
        m.start()
        block = ctx.enter_context(nc.Block())
        LOOPS = NT // 2

        def pipeline(eng, front, back, prepare=lambda: None):
            front(0, 0)
            prepare()

            def body(i, more):
                front(1, i)
                back(0, i)
                if more:
                    front(0, i + 1)
                back(1, i)

            body(0, True)
            with eng.Fori(1, LOOPS - 1) as i:
                body(i, True)
            body(LOOPS - 1, False)

        @block.sync
        def _(sp):
            def load_g(s, i):
                for q in range(2):
                    sp.dma_start(g[s][:, q * KB:(q + 1) * KB, :],
                                 scratch["mixed"][q * KB:(q + 1) * KB, :, bass.ds(i * (2 * P) + s * P, P)]
                                 .rearrange("b p t -> p b t")).then_inc(g_loaded[s][q], 16)

            def load_h(s, i):
                sp.dma_start(h[s][:, :], x[0, bass.ds(i * (2 * P) + s * P, P), :]).then_inc(h_loaded[s], 16)

            load_g(0, 0)
            sp.dma_start(gw[:, :], group_w).then_inc(gw_loaded, 16)
            for k in range(MB):
                if k >= STAGES:
                    sp.wait_ge(w_high, k - STAGES + 1 + START)
                    sp.wait_ge(w_low, k - STAGES + 1 + START)
                sp.dma_start(staging[k % STAGES][:, :], w_out[:, k, :]).then_inc(w_loaded[k % STAGES], 16)
                if k == KB:
                    load_g(1, 0)
            sp.wait_ge(w_high, MB + START)
            sp.wait_ge(w_low, MB + START)
            for s in range(2):
                load_h(s, 0)
            sp.dma_start(fw[:, :], final_w.to_broadcast([P, D])).then_inc(fw_loaded, 16)

            def reload_g(s, i):
                sp.wait_ge(g_high[s], i + 1 + START)
                sp.wait_ge(g_low[s], i + 1 + START)
                load_g(s, i + 1)

            def step(i, more):
                if more:
                    for s in range(2):
                        reload_g(s, i)
                for s in range(2):
                    sp.wait_ge(y_ready[s], i + 1 + START)
                    sp.dma_start(out[0, bass.ds(i * (2 * P) + s * P, P), :], y[s][:, :]).then_inc(stored[s], 16)
                    if more:
                        load_h(s, i + 1)

            with sp.Fori(0, LOOPS - 1) as i:
                step(i, True)
            step(LOOPS - 1, False)
            for s in range(2):
                sp.wait_ge(stored[s], 16 * LOOPS + START)

        @block.gpsimd
        def _(pool):
            nc.gpsimd.memset(ones[:, :], 1.0).then_inc(made, 1)
            nc.gpsimd.memset(power[:, :], -0.5).then_inc(made, 1)
            pool.wait_ge(made, START + 2)

            def back(s, i):
                pool.wait_ge(var_ready[s], i + 1 + START)
                nc.gpsimd.tensor_tensor(rstd[s][:, :], var[s][:, :], power[:, :], ALU.pow).then_inc(rstd_ready[s], 1)
                pool.wait_ge(f_var_ready[s], i + 1 + START)
                nc.gpsimd.tensor_tensor(f_rstd[s][:, :], f_var[s][:, :], power[:, 0:1], ALU.pow).then_inc(f_rstd_ready[s], 1)

            pipeline(pool, lambda s, i: None, back)

        @block.tensor
        def _(pe):
            pe.wait_ge(made, START + 2)

            def back(s, i):
                pe.wait_ge(var_ready[1 - s], i + s + START)
                for q in range(2):
                    pe.wait_ge(reduced[s][q], i + 1 + START)
                    last = nc.tensor.matmul(pss[:, q:q + 1], sq_sum[s][:, q, :], ones[:, :], start=True, stop=True)
                last.then_inc(ssq_ready[s], 1)
                pe.wait_ge(g_high[s], i + 1 + START)
                pe.wait_ge(g_low[s], i + 1 + START)

                def product(n, q, k):
                    for lhs, rhs in ((g_hi, w_hi), (g_hi, w_lo), (g_lo, w_hi)):
                        mm = nc.tensor.matmul(acc[n][q][:, :], lhs[s][:, k, :], rhs[:, k, n * W:(n + 1) * W],
                                              start=(k == q * KB and lhs is g_hi and rhs is w_hi),
                                              stop=(k == (q + 1) * KB - 1 and lhs is g_lo))
                    if k == (q + 1) * KB - 1:
                        mm.then_inc(acc_ready[s][n][q], 1)

                if isinstance(i, int) and i == 0 and s == 0:
                    for q in range(2):
                        for k in range(q * KB, (q + 1) * KB):
                            pe.wait_ge(w_high, k + 1 + START)
                            pe.wait_ge(w_low, k + 1 + START)
                            for n in range(NH):
                                product(n, q, k)
                else:
                    for n in range(NH):
                        pe.wait_ge(added[1 - s][n], i + s + START)
                        for q in range(2):
                            for k in range(q * KB, (q + 1) * KB):
                                product(n, q, k)

            pipeline(pe, lambda s, i: None, back)

        @block.scalar
        def _(act):
            def prepare():
                for k in range(MB):
                    act.wait_ge(w_loaded[k % STAGES], 16 * (k // STAGES + 1) + START)
                    nc.scalar.activation(w_hi[:, k, :], staging[k % STAGES][:, :], ACT.Copy).then_inc(w_high, 1)

            def front(s, i):
                for q in range(2):
                    act.wait_ge(g_loaded[s][q], i * 16 + 16 + START)
                    if q:
                        act.wait_ge(reduced[s][0], i + 1 + START)
                    else:
                        act.wait_ge(reduced[1 - s][1], i + s + START)
                    nc.scalar.activation(squares[:, :], g[s][:, q * KB:(q + 1) * KB, :].rearrange("p b t -> p (b t)"),
                                         ACT.Square).then_inc(squared[s][q], 1)
                act.wait_ge(weighed[s], i + 1 + START)
                act.wait_ge(acc_ready[s][NH - 1][1], i + START)
                nc.scalar.activation(g_hi[s][:, :, :], g[s][:, :, :], ACT.Copy).then_inc(g_high[s], 1)

            def back(s, i):
                act.wait_ge(added[s][NH - 1], i + 1 + START)
                nc.scalar.activation(h[s][:, :], y[s][:, :], ACT.Square,
                                     accum_out=f_ssq[s][:, :]).then_inc(f_ssq_ready[s], 1)

            pipeline(act, front, back, prepare)

        @block.vector
        def _(dve):
            def prepare():
                for k in range(MB):
                    dve.wait_ge(w_high, k + 1 + START)
                    nc.vector.tensor_tensor(w_lo[:, k, :], staging[k % STAGES][:, :], w_hi[:, k, :].bitcast(F32),
                                            ALU.subtract).then_inc(w_low, 1)

            dve.wait_ge(gw_loaded, START + 16)

            def front(s, i):
                for q in range(2):
                    dve.wait_ge(squared[s][q], i + 1 + START)
                    if q == 0:
                        dve.wait_ge(ssq_ready[s], i + START)
                    nc.vector.tensor_reduce(sq_sum[s][:, q, :], squares[:, :].rearrange("p (b t) -> p t b", b=KB),
                                            mybir.AxisListType.X, ALU.add).then_inc(reduced[s][q], 1)
                nc.vector.tensor_tensor(g[s][:, :, :], g[s][:, :, :], spread(gw[:, :], P), ALU.mult).then_inc(weighed[s], 1)
                dve.wait_ge(g_high[s], i + 1 + START)
                nc.vector.tensor_tensor(g_lo[s][:, :, :], g[s][:, :, :], g_hi[s][:, :, :].bitcast(F32),
                                        ALU.subtract).then_inc(g_low[s], 1)

            def back(s, i):
                dve.wait_ge(ssq_ready[s], i + 1 + START)
                nc.vector.tensor_scalar(var[s][:, :], pss[:, :], 1.0 / D, EPS, ALU.mult, ALU.add).then_inc(var_ready[s], 1)
                dve.wait_ge(rstd_ready[s], i + 1 + START)
                dve.wait_ge(h_loaded[s], i * 16 + 16 + START)
                dve.wait_ge(stored[s], i * 16 + START)
                for n in range(NH):
                    cols = slice(n * W, (n + 1) * W)
                    dve.wait_ge(acc_ready[s][n][0], i + 1 + START)
                    nc.vector.scalar_tensor_tensor(out=y[s][:, cols], in0=acc[n][0][:, :], scalar=rstd[s][:, 0:1],
                                                   in1=h[s][:, cols], op0=ALU.mult, op1=ALU.add).then_inc(half_added[s][n], 1)
                    dve.wait_ge(half_added[s][n], i + 1 + START)
                    dve.wait_ge(acc_ready[s][n][1], i + 1 + START)
                    nc.vector.scalar_tensor_tensor(out=y[s][:, cols], in0=acc[n][1][:, :], scalar=rstd[s][:, 1:2],
                                                   in1=y[s][:, cols], op0=ALU.mult, op1=ALU.add).then_inc(added[s][n], 1)
                dve.wait_ge(f_ssq_ready[s], i + 1 + START)
                nc.vector.tensor_scalar(f_var[s][:, :], f_ssq[s][:, :], 1.0 / D, EPS, ALU.mult,
                                        ALU.add).then_inc(f_var_ready[s], 1)
                dve.wait_ge(f_rstd_ready[s], i + 1 + START)
                if isinstance(i, int) and i == 0 and s == 0:
                    dve.wait_ge(fw_loaded, START + 16)
                nc.vector.scalar_tensor_tensor(out=y[s][:, :], in0=y[s][:, :], scalar=f_rstd[s][:, :], in1=fw[:, :],
                                               op0=ALU.mult, op1=ALU.mult).then_inc(y_ready[s], 1)

            pipeline(dve, front, back, prepare)


def hybrid_block(nc, x, meta, norm_w, w_blocks, w_dt, conv_wb, dt_cols, d_cols, group_w, w_out, final_w, out):
    shapes = {"k_hi": [PAIRS, P, T], "k_lo": [PAIRS, P, T], "q_hi": [PAIRS, P, SEQ], "q_lo": [PAIRS, P, SEQ],
              "xbc": [XB, P, T], "gate": [MB, P, SEQ], "v": [T, D], "mixed": [MB, P, SEQ]}
    scratch = {name: nc.dram_tensor(f"scratch_{name}", shape, F32, kind="Internal").ap() for name, shape in shapes.items()}
    with ExitStack() as ctx:
        dt_tok = ctx.enter_context(nc.sbuf_tensor("dt_tok", [P, NT + 1, 2, HEADS], F32))
        with ExitStack() as of_u:
            ut_hi = of_u.enter_context(nc.sbuf_tensor("ut_hi", [P, KB, T], F32R))
            ut_lo = of_u.enter_context(nc.sbuf_tensor("ut_lo", [P, KB, T], F32R))
            norm_stage(nc, x, meta, norm_w, ut_hi, ut_lo)
            feature_stage(nc, w_blocks, conv_wb, ut_hi, ut_lo, scratch)
            token_stage(nc, w_blocks, w_dt, dt_cols, ut_hi, ut_lo, dt_tok, scratch)
        with ExitStack() as of_state:
            state = of_state.enter_context(nc.sbuf_tensor("state", [P, GROUPS, W], F32))
            scan_start(nc, scratch, dt_tok, state)
            scan_stage(nc, scratch, d_cols, dt_tok, state)
    attention_stage(nc, scratch)
    output_stage(nc, scratch, x, w_out, group_w, final_w, out)


def kernel(x, meta_tokens, norm_w, w_in, conv_w, conv_b, dt_bias, a_log, d_skip, sb_norm_w, ssd_norm_w, w_out,
           final_norm_w):
    import numpy as np
    import concourse.bacc as bacc
    from concourse.bass_utils import run_bass_kernel_spmd

    def rows(a, b):
        return np.asarray(a).reshape(b, P).T

    w = np.asarray(w_in)[0]
    edges = np.cumsum([0, D, D, D, D, D, XBC, HEADS])
    q, k, v, sb_gate, z, xbc, dt = (w[:, a:b] for a, b in zip(edges[:-1], edges[1:]))

    def blocks(a):
        return a.reshape(KB, P, -1, P).transpose(2, 1, 0, 3)

    arrays = {
        "x": np.asarray(x),
        "meta": np.asarray(meta_tokens),
        "norm_w": rows(norm_w, KB),
        "w_blocks": np.concatenate([blocks(a) for a in (k, xbc, q, sb_gate, z, v)]),
        "w_dt": dt.reshape(KB, P, HEADS).transpose(1, 0, 2),
        "conv_wb": np.concatenate([np.asarray(conv_w)[0], np.asarray(conv_b)]).T.reshape(XB, P, CONV + 1),
        "dt_cols": np.stack([np.asarray(dt_bias)[0], np.asarray(a_log)[0]], axis=1),
        "d_cols": rows(np.repeat(np.asarray(d_skip)[0], HEAD), KB),
        "group_w": np.concatenate([rows(sb_norm_w, KB), rows(ssd_norm_w, KB)], axis=1),
        "w_out": np.asarray(w_out)[0].reshape(MB, P, D).transpose(1, 0, 2),
        "final_w": np.asarray(final_norm_w).reshape(1, D),
    }
    nc = bacc.Bacc("TRN2", target_bir_lowering=False, num_devices=1)
    args, feed = [], {}
    for name, array in arrays.items():
        feed[f"in_{name}"] = np.ascontiguousarray(array)
        args.append(nc.dram_tensor(f"in_{name}", array.shape, F32, kind="ExternalInput").ap())
    out = nc.dram_tensor("out_y", [1, SEQ, D], F32, kind="ExternalOutput").ap()
    hybrid_block(nc, *args, out)
    return run_bass_kernel_spmd(nc, [feed], core_ids=[0]).results[0]["out_y"]
```
